# Optimizing a Trainium2 kernel written in Bass

```python
import math, functools
import jax, jax.numpy as jnp
from jax import lax
import numpy as np

D_MODEL = 1024
BATCH = 1
SEQ = 2048
DEPTH = 2
DEC_BATCH = 8
DEC_SEQ = 4
PAST_LEN = 2048
PAGE_SIZE = 128

MIX_WIDTH = D_MODEL
RWKV_WIDTH = MIX_WIDTH // 2
RWKV_HEAD_DIM = 64
RWKV_HEADS = RWKV_WIDTH // RWKV_HEAD_DIM
DECAY_RANK = 64
ICLR_RANK = 64
DIFF_WIDTH = MIX_WIDTH - RWKV_WIDTH
DIFF_HEAD_DIM = 64
DIFF_K_DIM = 2 * DIFF_HEAD_DIM
DIFF_V_DIM = 2 * DIFF_HEAD_DIM
DIFF_HEADS = DIFF_WIDTH // DIFF_V_DIM
DIFF_QK = DIFF_HEADS * DIFF_K_DIM
SHIFT_COLS = 3 * RWKV_WIDTH + DECAY_RANK + ICLR_RANK
IN_COLS = SHIFT_COLS + RWKV_WIDTH + 2 * DIFF_QK + DIFF_WIDTH + DIFF_WIDTH
Q_BLOCK = 128
RMS_EPS = 1e-6
SUBLN_EPS = 1e-5
GN_EPS = 64e-5

kernel_name = "hymba_rwkv7_diffattn_step"

def rms_norm(x, w, eps):
    xf = x.astype(jnp.float32)
    y = xf * lax.rsqrt(jnp.mean(xf * xf, axis=-1, keepdims=True) + eps)
    return y * w.astype(jnp.float32)

def rwkv7_scan(S0, r, decay, k, v, a_vec, b_vec):
    def step(S, inp):
        r_t, w_t, k_t, v_t, a_t, b_t = inp
        sa = jnp.einsum('bhvk,bhk->bhv', S, a_t)
        S = S * w_t[:, :, None, :] + sa[..., None] * b_t[:, :, None, :] + v_t[..., None] * k_t[:, :, None, :]
        return S, jnp.einsum('bhvk,bhk->bhv', S, r_t)
    xs = tuple(jnp.swapaxes(t, 0, 1) for t in (r, decay, k, v, a_vec, b_vec))
    S, ys = lax.scan(step, S0, xs)
    return jnp.swapaxes(ys, 0, 1), S

def rwkv7_branch(cols, gate, prev_row, S0, shift_mu, decay_w0, decay_lora_b, iclr_a0, iclr_lora_b,
                 key_k, key_a, bonus_r_k, lnx_w, lnx_b):
    f32 = jnp.float32
    B, T, _ = cols.shape
    c = cols.astype(f32)
    shifted = jnp.concatenate([prev_row.astype(f32)[:, None, :], c[:, :-1, :]], axis=1)
    xs = c + (shifted - c) * shift_mu.astype(f32)
    W = RWKV_WIDTH
    r, k, v, xw, xa = jnp.split(xs, [W, 2 * W, 3 * W, 3 * W + DECAY_RANK], axis=-1)
    w = -jax.nn.softplus(-(decay_w0.astype(f32) + jnp.tanh(xw) @ decay_lora_b.astype(f32))) - 0.5
    decay = jnp.exp(-jnp.exp(w))
    a = jax.nn.sigmoid(iclr_a0.astype(f32) + xa @ iclr_lora_b.astype(f32))
    heads = lambda t: t.reshape(B, T, RWKV_HEADS, RWKV_HEAD_DIM)
    kk = heads(k * key_k.astype(f32))
    kk = kk / jnp.maximum(jnp.sqrt(jnp.sum(kk * kk, axis=-1, keepdims=True)), 1e-12)
    k = k * (1.0 + (a - 1.0) * key_a.astype(f32))
    r_h, k_h, v_h, d_h, a_h = heads(r), heads(k), heads(v), heads(decay), heads(a)
    y, S = rwkv7_scan(S0.astype(f32), r_h, d_h, k_h, v_h, -kk, kk * a_h)
    mu = jnp.mean(y, axis=-1, keepdims=True)
    var = jnp.mean(jnp.square(y - mu), axis=-1, keepdims=True)
    y = ((y - mu) * lax.rsqrt(var + GN_EPS)).reshape(B, T, W) * lnx_w.astype(f32) + lnx_b.astype(f32)
    bonus = jnp.sum(r_h * k_h * bonus_r_k.astype(f32), axis=-1, keepdims=True) * v_h
    y = y + bonus.reshape(B, T, W)
    return y * jax.nn.silu(gate.astype(f32)), S

def diff_lambda(lam_q1, lam_k1, lam_q2, lam_k2, lam_init):
    f = lambda p, q: jnp.exp(jnp.sum(p.astype(jnp.float32) * q.astype(jnp.float32)))
    return f(lam_q1, lam_k1) - f(lam_q2, lam_k2) + lam_init

def diff_attend(q, k, v, q_pos, k_pos, lam):
    s = jnp.einsum('bqhcd,bkhcd->bhcqk', q.astype(jnp.float32), k.astype(jnp.float32)) / math.sqrt(DIFF_HEAD_DIM)
    mask = k_pos[None, :] <= q_pos[:, None]
    s = jnp.where(mask, s, -jnp.inf)
    p = jax.nn.softmax(s, axis=-1)
    attn = p[:, :, 0] - lam * p[:, :, 1]
    return jnp.einsum('bhqk,bkhe->bqhe', attn, v.astype(jnp.float32))

def diff_prompt(q, k, v, lam):
    B, T = q.shape[:2]
    qb = min(Q_BLOCK, T)
    nb = T // qb
    q_blocks = jnp.swapaxes(q.reshape(B, nb, qb, DIFF_HEADS, 2, DIFF_HEAD_DIM), 0, 1)
    k_pos = jnp.arange(T)

    def one(args):
        q_blk, i = args
        return diff_attend(q_blk, k, v, i * qb + jnp.arange(qb), k_pos, lam)

    o = lax.map(one, (q_blocks, jnp.arange(nb)))
    return jnp.swapaxes(o, 0, 1).reshape(B, T, DIFF_HEADS, DIFF_V_DIM)

def diff_sample(q, k, v, lam, k_pool, v_pool, page_table):
    B, T = q.shape[:2]
    k_past = k_pool[page_table].reshape(B, -1, DIFF_HEADS, 2, DIFF_HEAD_DIM).astype(k.dtype)
    v_past = v_pool[page_table].reshape(B, -1, DIFF_HEADS, DIFF_V_DIM).astype(v.dtype)
    past = k_past.shape[1]
    k_all = jnp.concatenate([k_past, k], axis=1)
    v_all = jnp.concatenate([v_past, v], axis=1)
    return diff_attend(q, k_all, v_all, past + jnp.arange(T), jnp.arange(past + T), lam)

def mixer_layer(x, S0, prev_row, attend, lam_init, norm_w, w_in, shift_mu, decay_w0, decay_lora_b,
                iclr_a0, iclr_lora_b, key_k, key_a, bonus_r_k, lnx_w, lnx_b,
                lam_q1, lam_k1, lam_q2, lam_k2, subln_w, w_out):
    f32 = jnp.float32
    B, T, _ = x.shape
    h = rms_norm(x, norm_w, RMS_EPS).astype(x.dtype)
    proj = h @ w_in
    c0 = SHIFT_COLS
    c1 = c0 + RWKV_WIDTH
    c2 = c1 + DIFF_QK
    c3 = c2 + DIFF_QK
    c4 = c3 + DIFF_WIDTH
    rwkv_cols, rwkv_gate = proj[..., :c0], proj[..., c0:c1]
    q = proj[..., c1:c2].reshape(B, T, DIFF_HEADS, 2, DIFF_HEAD_DIM)
    k = proj[..., c2:c3].reshape(B, T, DIFF_HEADS, 2, DIFF_HEAD_DIM)
    v = proj[..., c3:c4].reshape(B, T, DIFF_HEADS, DIFF_V_DIM)
    diff_gate = proj[..., c4:]
    rwkv_out, S_new = rwkv7_branch(rwkv_cols, rwkv_gate, prev_row, S0, shift_mu, decay_w0, decay_lora_b,
                                   iclr_a0, iclr_lora_b, key_k, key_a, bonus_r_k, lnx_w, lnx_b)
    lam = diff_lambda(lam_q1, lam_k1, lam_q2, lam_k2, lam_init)
    o = attend(q, k, v, lam)
    o = rms_norm(o, subln_w, SUBLN_EPS) * (1.0 - lam_init)
    diff_out = o.reshape(B, T, DIFF_WIDTH) * jax.nn.silu(diff_gate.astype(f32))
    mixed = jnp.concatenate([rwkv_out, diff_out], axis=-1).astype(x.dtype)
    x_new = x + mixed @ w_out
    return x_new, S_new, rwkv_cols[:, -1, :], k.reshape(B, T, DIFF_HEADS, DIFF_K_DIM), v

def setup_inputs(seed: int = 0) -> dict:
    key = jax.random.key(seed)
    ks = jax.random.split(key, 32)
    f32 = jnp.float32
    nrm = lambda kk, shape, s=1.0: s * jax.random.normal(kk, shape, f32)
    n_pages = PAST_LEN // PAGE_SIZE
    n_used = DEC_BATCH * n_pages
    n_phys = n_used + max(1, n_used // 4)
    perm = jax.random.permutation(ks[4], n_phys)
    page_table = perm[:n_used].reshape(DEC_BATCH, n_pages).astype(jnp.int32)
    return {
        'x_prompt': nrm(ks[0], (BATCH, SEQ, D_MODEL)),
        'x_sample': nrm(ks[1], (DEC_BATCH, DEC_SEQ, D_MODEL)),
        'cache_k': nrm(ks[2], (DEPTH, n_phys, PAGE_SIZE, DIFF_HEADS, DIFF_K_DIM)),
        'cache_v': nrm(ks[3], (DEPTH, n_phys, PAGE_SIZE, DIFF_HEADS, DIFF_V_DIM)),
        'page_table': page_table,
        'state_rwkv': nrm(ks[5], (DEPTH, DEC_BATCH, RWKV_HEADS, RWKV_HEAD_DIM, RWKV_HEAD_DIM), 0.3),
        'state_shift': nrm(ks[6], (DEPTH, DEC_BATCH, SHIFT_COLS)),
        'norm_w': 1.0 + nrm(ks[7], (DEPTH, D_MODEL), 0.02),
        'w_in': nrm(ks[8], (DEPTH, D_MODEL, IN_COLS), D_MODEL ** -0.5),
        'shift_mu': jax.random.uniform(ks[9], (DEPTH, SHIFT_COLS), f32),
        'decay_w0': -3.0 + nrm(ks[10], (DEPTH, RWKV_WIDTH)),
        'decay_lora_b': nrm(ks[11], (DEPTH, DECAY_RANK, RWKV_WIDTH), 0.1 * DECAY_RANK ** -0.5),
        'iclr_a0': nrm(ks[12], (DEPTH, RWKV_WIDTH), 0.1),
        'iclr_lora_b': nrm(ks[13], (DEPTH, ICLR_RANK, RWKV_WIDTH), 0.5 * ICLR_RANK ** -0.5),
        'key_k': 0.85 + nrm(ks[14], (DEPTH, RWKV_WIDTH), 0.02),
        'key_a': 1.0 + nrm(ks[15], (DEPTH, RWKV_WIDTH), 0.02),
        'bonus_r_k': nrm(ks[16], (DEPTH, RWKV_HEADS, RWKV_HEAD_DIM), 0.1),
        'lnx_w': 1.0 + nrm(ks[17], (DEPTH, RWKV_WIDTH), 0.02),
        'lnx_b': nrm(ks[18], (DEPTH, RWKV_WIDTH), 0.02),
        'lam_q1': nrm(ks[19], (DEPTH, DIFF_HEAD_DIM), 0.1),
        'lam_k1': nrm(ks[20], (DEPTH, DIFF_HEAD_DIM), 0.1),
        'lam_q2': nrm(ks[21], (DEPTH, DIFF_HEAD_DIM), 0.1),
        'lam_k2': nrm(ks[22], (DEPTH, DIFF_HEAD_DIM), 0.1),
        'subln_w': 1.0 + nrm(ks[23], (DEPTH, DIFF_V_DIM), 0.02),
        'w_out': nrm(ks[24], (DEPTH, MIX_WIDTH, D_MODEL), MIX_WIDTH ** -0.5),
        'final_norm_w': 1.0 + nrm(ks[25], (D_MODEL,), 0.02),
    }

def reference(x_prompt, x_sample, cache_k, cache_v, page_table, state_rwkv, state_shift,
              norm_w, w_in, shift_mu, decay_w0, decay_lora_b, iclr_a0, iclr_lora_b, key_k, key_a,
              bonus_r_k, lnx_w, lnx_b, lam_q1, lam_k1, lam_q2, lam_k2, subln_w, w_out, final_norm_w):
    xp, xs = x_prompt, x_sample
    Bp = x_prompt.shape[0]
    kp_l, vp_l, sp_l, hp_l = [], [], [], []
    ks_l, vs_l, ss_l, hs_l = [], [], [], []
    for l in range(DEPTH):
        lam_init = 0.8 - 0.6 * math.exp(-0.3 * l)
        lp = (norm_w[l], w_in[l], shift_mu[l], decay_w0[l], decay_lora_b[l], iclr_a0[l], iclr_lora_b[l],
              key_k[l], key_a[l], bonus_r_k[l], lnx_w[l], lnx_b[l],
              lam_q1[l], lam_k1[l], lam_q2[l], lam_k2[l], subln_w[l], w_out[l])
        S0p = jnp.zeros((Bp, RWKV_HEADS, RWKV_HEAD_DIM, RWKV_HEAD_DIM), jnp.float32)
        prev0p = jnp.zeros((Bp, SHIFT_COLS), xp.dtype)
        xp, Sp, hp, kp, vp = mixer_layer(xp, S0p, prev0p, diff_prompt, lam_init, *lp)
        attend_s = functools.partial(diff_sample, k_pool=cache_k[l], v_pool=cache_v[l], page_table=page_table)
        xs, Ss, hs, kss, vss = mixer_layer(xs, state_rwkv[l], state_shift[l], attend_s, lam_init, *lp)
        kp_l.append(kp)
        vp_l.append(vp)
        sp_l.append(Sp.astype(x_prompt.dtype))
        hp_l.append(hp)
        ks_l.append(kss)
        vs_l.append(vss)
        ss_l.append(Ss.astype(state_rwkv.dtype))
        hs_l.append(hs.astype(state_shift.dtype))
    y_prompt = rms_norm(xp, final_norm_w, RMS_EPS).astype(x_prompt.dtype)
    y_sample = rms_norm(xs, final_norm_w, RMS_EPS).astype(x_sample.dtype)
    k_prompt = jnp.stack(kp_l, 0)
    v_prompt = jnp.stack(vp_l, 0)
    rwkv_prompt = jnp.stack(sp_l, 0)
    shift_prompt = jnp.stack(hp_l, 0)
    k_sample = jnp.stack(ks_l, 0)
    v_sample = jnp.stack(vs_l, 0)
    rwkv_sample = jnp.stack(ss_l, 0)
    shift_sample = jnp.stack(hs_l, 0)
    return (y_prompt, y_sample, k_prompt, v_prompt, rwkv_prompt, shift_prompt,
            k_sample, v_sample, rwkv_sample, shift_sample)


_drawn_inputs = setup_inputs


def setup_inputs(seed=0):
    import zlib

    import numpy as np

    out = dict(_drawn_inputs(seed))
    spreads = {}
    factors = {'decay_lora_b': 8.0,
     'key_k': 10.79,
     'lnx_w': 5.13,
     'lnx_b': 12.673,
     'lam_k1': 4.07,
     'lam_q2': 2.872,
     'subln_w': 6.439,
     'final_norm_w': 7.841}
    for name, (base, spread) in spreads.items():
        noise = np.random.default_rng([zlib.crc32(name.encode()), seed]).standard_normal(out[name].shape)
        drawn = base * np.exp(spread * noise) if base else spread * noise
        out[name] = __import__('jax').numpy.asarray(drawn.astype(out[name].dtype))
    for name, factor in factors.items():
        out[name] = (out[name] * factor).astype(out[name].dtype)
    return out
```

```python
import math
from contextlib import ExitStack

import concourse.bass as bass
from concourse import mybir
from concourse.alu_op_type import AluOpType as ALU

ACT = mybir.ActivationFunctionType
AX = mybir.AxisListType
F32 = mybir.dt.float32
F32R = mybir.dt.float32r
I32 = mybir.dt.int32

P = 128
ARENA = 49000
D = 1024
KT = D // P
SEQ = 2048
NS = 32
TOK = SEQ + NS
DEPTH = 2
COLS = 4224
CB = COLS // P
NT = SEQ // P
GRP = 512
RMS_EPS = 1e-6
GN_EPS = 64e-5
RW = 512
TG = 416
CH = 64
NC = GRP // CH
C_LINKS = 2 * NT + 2 * NT + 5

LEVELS = (2, 4, 8, 16, 32)
DECAY = math.exp(-0.5)
HEADS = 4
SUBLN_EPS = 1e-5
ORDER = [t for i in range(NT // 2) for t in (i, NT - 1 - i)]
BLOCKS = [i // 4 + 1 for i in ORDER]
FIRST = [sum(BLOCKS[:i]) for i in range(NT + 1)]
Q_ROW, K_ROW, V_ROW, DG_ROW = 2176, 2688, 3200, 3712
NEG = -1e30
N_PHYS = 160
GATE_ROW = 3 * RW + 2 * 64


class Mark:

    def __init__(self, sem, per, unit=1, credit=0):
        self.sem, self.per, self.unit, self.credit, self.j = sem, per, unit, credit, 0

    def inc(self, ins):
        ins.then_inc(self.sem, self.unit)
        self.j += 1

    def link(self, eng, n, ins):
        self.inc(ins)
        self.wait(eng, n, self.j)

    def wait(self, eng, n, j):
        assert 0 < j <= self.per
        eng.wait_ge(self.sem, (n * self.per + j + self.credit) * self.unit)
        if eng is Mark.pe and not isinstance(n, int):
            eng.sem_inc(Mark.tick, 1)

    def wait_before(self, eng, n):
        assert self.credit
        eng.wait_ge(self.sem, (n * self.per + self.credit) * self.unit)

    def wait_ge(self, eng, n, j):
        if isinstance(n, int) and n == 0:
            return
        eng.wait_ge(self.sem, ((n - 1) * self.per + j) * self.unit)

    def grant(self, eng):
        eng.sem_inc(self.sem, self.credit * self.unit)

    def close(self):
        assert self.j == self.per, (self.sem, self.j, self.per)
        self.j = 0


class Phases:

    def __init__(self, nc, arrive, go, tick, clear, per_layer):
        self.nc, self.arrive, self.go, self.tick, self.clear, self.per_layer = nc, arrive, go, tick, clear, per_layer

    def end(self, eng, l, k, leader=False):
        n = l * self.per_layer + (k + 1)
        eng.sem_inc(self.tick, 1)
        eng.drain()
        if leader:
            eng.wait_ge(self.arrive, n * 4)
            eng.sem_inc(self.tick, 1)
            for s in self.clear[k]:
                eng.sem_clear(s)
            eng.drain()
            eng.sem_inc(self.go, 1)
        else:
            eng.sem_inc(self.arrive, 1)
            eng.wait_ge(self.go, n)
            eng.sem_inc(self.tick, 1)


def build(nc, ins, outs):
    x_in, w_in, norm_w = ins["x"], ins["w_in"], ins["norm_w"]
    xcur = nc.dram_tensor("x_cur", (TOK, D), F32, kind="Internal").ap()
    PT = outs["proj_t"]
    ctx = ExitStack()
    with ctx:
        def sb(name, shape, dt=F32):
            return ctx.enter_context(nc.sbuf_tensor(name, shape, dt))

        def ps(name, shape, dt=F32):
            return ctx.enter_context(nc.psum_tensor(name, shape, dt))

        def sem(name):
            return ctx.enter_context(nc.semaphore(name))

        psum = ps("psum", [P, 8, 512])
        shared, used = [], [0]

        def phase_sems():
            used[0] = 0

        def psem(name):
            if used[0] == len(shared):
                shared.append(sem(f"phase_sem{used[0]}"))
            used[0] += 1
            return shared[used[0] - 1]

        bank = [psum[:, i, :] for i in range(8)]
        ident = sb("ident", [P, P])
        eps_rms, eps_gn = sb("eps_rms", [P, 1]), sb("eps_gn", [P, 1])
        with nc.sbuf_tensor("h_parts", [P, 2, KT, TOK], F32R) as h_parts, nc.sbuf_tensor("w_parts", [P, 3, 2, KT, P], F32R) as w_parts:
            split_a = 2 * KT * TOK + 6 * KT * P
        arena = sb("arena", [P, ARENA])

        class Carve:

            def __init__(self):
                self.at = 0

            def __call__(self, *dims):
                n = math.prod(dims)
                v = arena[:, self.at:self.at + n]
                self.at += n
                assert self.at <= ARENA, self.at
                if len(dims) == 1:
                    return v
                names = "abcd"[:len(dims)]
                return v.rearrange("p (%s) -> p %s" % (" ".join(names), " ".join(names)), **dict(zip(names, dims)))

        cv = Carve()
        h_hi, h_lo = h_parts[:, 0], h_parts[:, 1]
        w_hi, w_lo = [[w_parts[:, u, i] for u in range(3)] for i in range(2)]
        cv.at = split_a
        nw = cv(KT)
        resident = cv.at
        xt, ht = cv(4, D), cv(2, D)
        sqj, st = cv(D), cv(3, 4)
        cv.at = resident
        wb = [cv(KT, P) for _ in range(3)]
        ost = [cv(TOK + 1) for _ in range(3)]

        c_ld, c_x, c_eps, p_z = sem("c_ld"), sem("c_x"), sem("c_eps"), sem("p_z")
        arrive, go, tick = sem("arrive"), sem("go"), sem("tick")
        a_xs = [sem(f"a_x{i}") for i in range(4)]
        a_ssq, a_var, a_rstd, a_h, a_tr, a_ev, a_nw = [sem("a_" + n) for n in ("ssq", "var", "rstd", "h", "tr", "ev", "nw")]
        p_w = [sem(f"p_w{i}") for i in range(3)]
        a_hi, p_w1, p_ws = sem("a_hi"), sem("p_wprod"), sem("p_wsplit")
        p_mm, p_evA, p_evD = sem("p_mm"), sem("p_evA"), sem("p_evD")
        p_st = [sem(f"p_st{i}") for i in range(3)]
        MT = nc.dram_tensor("mixed_t", (D, TOK), F32, kind="Internal").ap()
        cv = Carve()
        phase_sems()
        bd0 = cv.at
        B_bd, K_bd, R_bd = cv(NC, P), cv(NC, P), cv(2, NC, P)
        SMB, SMK = cv(NC, 2, P), cv(NC, 2, P)
        A_tok, Bh_tok, Kh_tok = cv(NC, P), cv(NC, P), cv(NC, P)
        bd_zero = arena[:, bd0:cv.at]
        prm, dpr, lwp = cv(4, 16), cv(4, 8), cv(4, 2, P)
        raw, rawl, gate, lin = cv(3, GRP + 1), cv(GRP + 1), cv(GRP), cv(GRP)
        cop, xk, xr = cv(4, GRP), cv(GRP), cv(GRP)
        ld, ta, L = cv(GRP), cv(GRP), cv(GRP)
        E, Ei = cv(2, NC, CH + 1), cv(GRP)
        kkr, kks, rn, kkn, kf, bb, rkb = [cv(GRP) for _ in range(7)]
        bv, sg = cv(2, GRP), cv(2, GRP)
        RAV, BKh, kst = cv(NC, 3, CH), cv(NC, 2, CH), cv(2, GRP)
        X, XT, Yl = cv(NC, P), cv(NC, P), cv(NC, P)
        V_tok, MV, Uv, U, WT = cv(NC, CH), cv(NC, CH), cv(NC, CH), cv(NC, CH), cv(NC, P)
        Z = cv(4, 2, CH)
        yc, ysq, ysb, mix = cv(GRP), cv(GRP), cv(GRP), cv(GRP)
        fst = cv(4, NC)
        mS, mR, mX1, mL, ones_b = cv(P), cv(GRP), cv(P), cv(len(LEVELS), P), cv(P)
        r_sems = []

        def mark(name, per, unit=1, credit=0):
            m = Mark(psem("r_" + name), per, unit, credit)
            r_sems.append(m.sem)
            return m
        NL = len(LEVELS)
        r_cst, r_in, r_inl, r_g, r_out = [mark(n, 1, 16).sem for n in ("cst", "in", "in_lora", "in_gate", "out")]
        r_once = mark("once", 1).sem
        free_raw, free_lora = mark("raw_free", 1, credit=1), mark("lora_free", 1, credit=1)
        sA_CK, sA_CR, sA_CV, sA_TG, sA_TW, sA_TA, sA_E, sA_EI, sA_NRM = range(1, 10)
        sD_XK, sD_XR, sD_XV, sD_SG, sD_LD, sD_SCAN, sD_KF1, sD_KF2, sD_RKB, sD_MAX, sD_REC1, sD_REC2, sD_KKN, sD_A, sD_BB, sD_B0, sD_B1, sD_BV = range(1, 19)
        sG_KKR, sG_SQ, sG_R, sG_RB, sG_K0, sG_K1, sG_BH, sG_BV = range(1, 9)
        sP_ZW, sP_ZA, sP_SS, sP_BO = range(1, 5)
        pA, pD, pG, pP = mark("prep_scalar", 9), mark("prep_vector", 18), mark("prep_gpsimd", 8), mark("prep_tensor", 4)
        lA, lD = mark("lora_scalar", 2), mark("lora_vector", 1)
        scB, tAV, scK, tBK = mark("scores_b", 2), mark("turned_av", 1), mark("scores_k", 2), mark("turned_bk", 1)
        smB, kcp, smK = mark("masked_b", 2), mark("copied_k", 2), mark("masked_k", 2)
        x0t, xx, xt_ok = mark("xt_first", 4), mark("x_added", 2 * NL), mark("xt_copied", 2 * NL)
        avE, bkE = mark("av_out", 1), mark("bk_out", 1)
        yP, yD, xP, tP = mark("y_made", 2 * NL), mark("y_masked", 2 * NL), mark("x_made", 2 * NL), mark("x_turned", 2 * NL)
        mvP, mvA, wtP, wtA, uvP, uvA = [mark(n, 1) for n in ("mv_made", "mv_out", "wt_made", "wt_out", "uv_made", "uv_out")]
        uP, uD, zP, zD, yAll = mark("u_made", NC), mark("u_summed", NC), mark("z_made", NC), mark("z_new", NC), mark("y_all", 1)
        F_SUM, F_NEG, F_YC, F_VAR, F_REC, F_YN, F_Y2, F_MIX = range(1, 9)
        fD, fA, fP = mark("post_vector", 8), mark("post_scalar", 4), mark("post_tensor", 1)
        FA_SQ, FA_RT, FA_C0, FA_C1 = range(1, 5)
        hs = lambda h: slice(64 * h, 64 * h + 64)
        c8 = lambda v: v.rearrange("p (c t) -> p c t", c=NC)
        c4b = lambda g: bank[g].rearrange("p (c t) -> p c t", c=4)
        gq = lambda g: slice(4 * g, 4 * g + 4)

        def units(eng, pair):
            pair(None, (0, 0, 0))
            with eng.Fori(0, 3) as tg:
                for cb in range(4):
                    pair((tg * 4 + cb, cb, tg), (tg * 4 + (cb + 1), (cb + 1) % 4, tg + (cb + 1) // 4))
            for cb in range(4):
                pair((12 + cb, cb, 3), (13 + cb, cb + 1, 3) if cb < 3 else None)

        def dyn(start, n):
            return slice(start, start + n) if isinstance(start, int) else bass.ds(start, n)

        def rwkv_sync(sp, l):
            for dst, src in ((mS, "mS"), (mR, "mR"), (mX1, "mX1"), (mL, "mL"), (ones_b, "ones_b")):
                sp.dma_start(dst, ins[src]).then_inc(r_cst, 16)
            sp.dma_start(prm[:, :, :], ins["prm"][bass.ds(l * 4, 4)].rearrange("c p k -> p c k")).then_inc(r_cst, 16)
            sp.dma_start(lwp[:, :, :, :], ins["lorap"][bass.ds(l, 1)].rearrange("l p c a k -> (l p) c a k")).then_inc(r_cst, 16)

            def pair(s_, p_):
                if p_ is None:
                    return
                n, cb, tg = p_
                if cb == 0:
                    free_lora.wait_before(sp, tg)
                    sp.dma_start(rawl[:, :], PT[bass.ds(l * COLS + 12 * P, P), dyn(tg * GRP, GRP + 1)]).then_inc(r_inl, 16)
                free_raw.wait_before(sp, n)
                for j in (1, 0, 2):
                    sp.dma_start(raw[:, j, :], PT[bass.ds(l * COLS + (j * RW + cb * P), P), dyn(tg * GRP, GRP + 1)]).then_inc(r_in, 16)
                pD.wait_ge(sp, n, sD_SG)
                sp.dma_start(gate[:, :], PT[bass.ds(l * COLS + (GATE_ROW + cb * P), P), dyn(tg * GRP + 1, GRP)]).then_inc(r_g, 16)
            units(sp, pair)

        def rwkv_scalar(act, l):
            act.wait_ge(r_once, 4)

            def prep(p_):
                n, cb, tg = p_
                if cb == 0:
                    act.wait_ge(r_inl, (tg + 1) * 16)
                    lA.inc(act.activation(cop[:, 3, :], rawl[:, 1:GRP + 1], ACT.Copy, scale=dpr[:, 0, 3:4]))
                act.wait_ge(r_in, (n + 1) * 48)
                for j in (1, 0, 2):
                    pA.inc(act.activation(cop[:, j, :], raw[:, j, 1:GRP + 1], ACT.Copy, scale=dpr[:, cb, j:j + 1]))
                if cb == 0:
                    lD.wait(act, tg, 1)
                    lA.inc(act.activation(lin[0:64, :], lin[0:64, :], ACT.Tanh))
                    lA.close()
                act.wait_ge(r_g, (n + 1) * 16)
                pA.inc(act.activation(sg[:, cb % 2, :], gate[:, :], ACT.Tanh, scale=0.5))
                pP.wait(act, n, sP_ZW)
                pA.inc(act.activation(ld[:, :], bank[4], ACT.Tanh, bias=dpr[:, cb, 4:5], scale=0.5))
                pP.wait(act, n, sP_ZA)
                pA.inc(act.activation(ta[:, :], bank[5], ACT.Tanh, bias=dpr[:, cb, 5:6], scale=0.5))
                pD.wait(act, n, sD_SCAN)
                pA.inc(act.activation(E[:, cb % 2, :, 1:CH + 1], c8(L[:, :]), ACT.Exp))
                pA.inc(act.activation(Ei[:, :], L[:, :], ACT.Exp, scale=-1.0))
                pP.wait(act, n, sP_SS)
                pA.inc(act.activation(rn[:, :], bank[6], ACT.Sqrt))
                pA.close()

            def post(s_, k):
                n, cb, tg = s_
                if k == 0:
                    fD.wait(act, n, F_YC)
                    fA.inc(act.activation(ysq[:, :], yc[:, :], ACT.Square))
                elif k == 1:
                    fD.wait(act, n, F_VAR)
                    fA.inc(act.activation(fst[:, 2, :], fst[:, 1, :], ACT.Sqrt, bias=eps_gn[:, :], scale=1.0 / CH))
                elif k == 2:
                    fP.wait(act, n, 1)
                    for h in range(2):
                        fA.inc(act.activation(c8(ysb[hs(h), :]), psum[0:64, 6:8, :].rearrange("p b (c q) -> p (b c) q", c=4)[:, :, hs(h)], ACT.Copy))
                    fA.close()
                elif k == 3:
                    fD.wait(act, n, F_MIX)
                    act.dma_start(MT[cb * P:(cb + 1) * P, dyn(tg * GRP, GRP)], mix[:, :]).then_inc(r_out, 16)

            def pair(s_, p_):
                if p_:
                    prep(p_)
                    n = p_[0]
                    scK.wait(act, n, 1)
                    kcp.inc(act.activation(kst[:, 0, :], bank[2], ACT.Copy))
                    for g in range(2):
                        tP.wait(act, n, g + 1)
                        xt_ok.inc(act.activation(X[:, gq(g), :], c4b(g), ACT.Copy))
                    scK.wait(act, n, 2)
                    kcp.inc(act.activation(kst[:, 1, :], bank[3], ACT.Copy))
                    tAV.wait(act, n, 1)
                    tw4 = psum[:, 4:6, :].rearrange("p b (c q) -> p (b c) q", c=4)
                    act.activation(A_tok[0:64, :, 0:64], tw4[0:64, :, 0:64], ACT.Copy)
                    act.activation(A_tok[64:128, :, 64:128], tw4[0:64, :, 64:128], ACT.Copy)
                    act.activation(V_tok[0:64, :, :], tw4[64:128, :, 0:64], ACT.Copy)
                    avE.inc(act.activation(V_tok[64:128, :, :], tw4[64:128, :, 64:128], ACT.Copy))
                if s_:
                    post(s_, 0)
                    post(s_, 1)
                if p_:
                    tBK.wait(act, n, 1)
                    tw6 = psum[:, 6:8, :].rearrange("p b (c q) -> p (b c) q", c=4)
                    act.activation(Bh_tok[0:64, :, 0:64], tw6[0:64, :, 0:64], ACT.Copy)
                    act.activation(Bh_tok[64:128, :, 64:128], tw6[0:64, :, 64:128], ACT.Copy)
                    act.activation(Kh_tok[0:64, :, 0:64], tw6[64:128, :, 0:64], ACT.Copy)
                    bkE.inc(act.activation(Kh_tok[64:128, :, 64:128], tw6[64:128, :, 64:128], ACT.Copy))
                    mvP.wait(act, n, 1)
                    mvA.inc(act.activation(MV[:, :, :], c8(bank[4]), ACT.Copy))
                    for v in range(NL - 1):
                        for g in range(2):
                            tP.wait(act, n, 2 * v + g + 3)
                            xt_ok.inc(act.activation(XT[:, gq(g), :], c4b(g), ACT.Copy))
                        if v == 1 and s_:
                            post(s_, 2)
                    wtP.wait(act, n, 1)
                    for g in range(2):
                        w_ = act.activation(WT[:, gq(g), :], c4b(g), ACT.Copy)
                    wtA.inc(w_)
                    uvP.wait(act, n, 1)
                    uvA.inc(act.activation(Uv[:, :, :], c8(bank[5]), ACT.Copy))
                    for m in (kcp, xt_ok, avE, bkE, mvA, wtA, uvA):
                        m.close()
                elif s_:
                    post(s_, 2)
                if s_:
                    post(s_, 3)
            units(act, pair)
            for c in range(4):
                act.dma_start(outs["sp"][bass.ds(l * RW + c * P, P), :], Z[:, c, 0, :]).then_inc(r_out, 16)
            act.wait_ge(r_out, 16 * 21)

        def rwkv_gpsimd(pool, l):
            pool.memset(bd_zero[:, :], 0.0).then_inc(r_once, 1)
            pool.wait_ge(r_once, 4)
            pool.memset(E[:, :, :, 0:1], 1.0)

            def pair(s_, p_):
                if p_ is None:
                    return
                n, cb, tg = p_
                q = cb % 2
                smK.wait_ge(pool, n, 2)
                pD.wait(pool, n, sD_XK)
                pG.link(pool, n, pool.tensor_tensor(kkr[:, :], xk[:, :], prm[:, cb, 6:7].to_broadcast([P, GRP]), ALU.mult))
                pG.inc(pool.tensor_tensor(kks[:, :], kkr[:, :], kkr[:, :], ALU.mult))
                pA.wait(pool, n, sA_E)
                pG.link(pool, n, pool.tensor_tensor(RAV[:, :, 0, :], c8(xr[:, :]), E[:, q, :, 1:CH + 1], ALU.mult))
                for h in range(2):
                    r_ = pool.tensor_tensor(R_bd[hs(h), q, :, hs(h)], c8(xr[hs(h), :]), E[hs(h), q, :, 1:CH + 1], ALU.mult)
                pG.inc(r_)
                pA.wait(pool, n, sA_EI)
                pD.wait(pool, n, sD_KF2)
                for h in range(2):
                    pG.inc(pool.tensor_tensor(K_bd[hs(h), :, hs(h)], c8(kf[hs(h), :]), c8(Ei[hs(h), :]), ALU.mult))
                pG.wait(pool, n, sG_K1)
                pD.wait(pool, n, sD_B1)
                for h in range(2):
                    pe_ = E[hs(h), q, :, CH:CH + 1].to_broadcast([64, NC, CH])
                    pool.tensor_tensor(BKh[hs(h), :, 0, :], B_bd[hs(h), :, hs(h)], pe_, ALU.mult)
                    b_ = pool.tensor_tensor(BKh[hs(h), :, 1, :], K_bd[hs(h), :, hs(h)], pe_, ALU.mult)
                pG.link(pool, n, b_)
                pD.wait(pool, n, sD_BV)
                pG.link(pool, n, pool.tensor_tensor(bv[:, q, :], bv[:, q, :], prm[:, cb, 10:11].to_broadcast([P, GRP]), ALU.add))
                pG.close()
                for g in range(2):
                    kcp.wait(pool, n, g + 1)
                    for h in range(2):
                        k_ = pool.tensor_tensor(SMK[hs(h), gq(g), :, hs(h)], kst[hs(h), g, :].rearrange("p (c x t) -> p c x t", c=4, x=2),
                                                mS[hs(h), :].rearrange("p (x t) -> p x t", x=2).unsqueeze(1).to_broadcast([64, 4, 2, 64]), ALU.mult)
                    smK.inc(k_)
                smK.close()
            units(pool, pair)

        def rwkv_vector(dve, l):
            free_raw.grant(dve)
            free_lora.grant(dve)
            dve.sem_inc(r_out, 16)
            dve.wait_ge(r_cst, 16 * 7)
            dve.memset(Z[:, :, :, :], 0.0)
            dve.tensor_scalar(dpr[:, :, 0:4], prm[:, :, 0:4], -1.0, 1.0, ALU.mult, ALU.add).then_inc(r_once, 1)
            dve.tensor_scalar(dpr[:, :, 4:6], prm[:, :, 4:6], 0.5, None, ALU.mult).then_inc(r_once, 1)
            dve.tensor_scalar(dpr[:, :, 6:7], prm[:, :, 7:8], 0.5, None, ALU.mult).then_inc(r_once, 1)
            dve.wait_ge(r_once, 4)

            def prep(p_, k):
                n, cb, tg = p_
                q = cb % 2

                def mixed(out, j, mu, prev):
                    pA.wait(dve, n, j)
                    return dve.scalar_tensor_tensor(out, prev, prm[:, cb, mu:mu + 1], cop[:, mu, :], ALU.mult, ALU.add)
                if k == sD_XK:
                    if cb == 0:
                        lA.wait(dve, tg, 1)
                        lD.inc(dve.scalar_tensor_tensor(lin[:, :], rawl[:, 0:GRP], prm[:, 0, 3:4], cop[:, 3, :], ALU.mult, ALU.add))
                        lD.wait(dve, tg, 1)
                        dve.sem_inc(free_lora.sem, 1)
                        lD.close()
                    i_ = mixed(xk[:, :], sA_CK, 1, raw[:, 1, 0:GRP])
                elif k == sD_XR:
                    i_ = mixed(xr[:, :], sA_CR, 0, raw[:, 0, 0:GRP])
                elif k == sD_XV:
                    pA.wait(dve, n, sA_CV)
                    i_ = dve.scalar_tensor_tensor(RAV[:, :, 2, :], c8(raw[:, 2, 0:GRP]), prm[:, cb, 2:3], c8(cop[:, 2, :]), ALU.mult, ALU.add)
                elif k == sD_SG:
                    pD.wait(dve, n, sD_XV)
                    dve.sem_inc(free_raw.sem, 1)
                    pA.wait(dve, n, sA_TG)
                    i_ = dve.scalar_tensor_tensor(sg[:, q, :], sg[:, q, :], 1.0, gate[:, :], ALU.add, ALU.mult)
                elif k == sD_LD:
                    pA.wait(dve, n, sA_TW)
                    i_ = dve.tensor_scalar(ld[:, :], ld[:, :], 1.0, -0.5 * DECAY, ALU.add, ALU.mult)
                elif k == sD_SCAN:
                    pD.wait(dve, n, sD_LD)
                    i_ = dve.tensor_tensor_scan(L[:, :], mR[:, :], ld[:, :], 0.0, ALU.mult, ALU.add)
                elif k == sD_KF1:
                    pA.wait(dve, n, sA_TA)
                    i_ = dve.tensor_scalar(kf[:, :], ta[:, :], 1.0, dpr[:, cb, 6:7], ALU.subtract, ALU.mult)
                elif k == sD_KF2:
                    pD.wait(dve, n, sD_KF1)
                    i_ = dve.scalar_tensor_tensor(kf[:, :], kf[:, :], 1.0, xk[:, :], ALU.add, ALU.mult)
                elif k == sD_RKB:
                    pD.wait(dve, n, sD_KF2)
                    i_ = dve.scalar_tensor_tensor(rkb[:, :], xr[:, :], prm[:, cb, 8:9], kf[:, :], ALU.mult, ALU.mult)
                elif k == sD_MAX:
                    pA.wait(dve, n, sA_NRM)
                    i_ = dve.tensor_scalar(rn[:, :], rn[:, :], 1e-12, None, ALU.max)
                elif k in (sD_REC1, sD_REC2):
                    pD.wait(dve, n, sD_MAX)
                    w = slice(0, 256) if k == sD_REC1 else slice(256, 512)
                    i_ = dve.reciprocal(rn[:, w], rn[:, w])
                elif k == sD_KKN:
                    pD.wait(dve, n, sD_REC2)
                    i_ = dve.tensor_tensor(kkn[:, :], kkr[:, :], rn[:, :], ALU.mult)
                elif k == sD_A:
                    pD.wait(dve, n, sD_KKN)
                    i_ = dve.scalar_tensor_tensor(RAV[:, :, 1, :], c8(kkn[:, :]), -1.0, E[:, q, :, 0:CH], ALU.mult, ALU.mult)
                elif k == sD_BB:
                    i_ = dve.scalar_tensor_tensor(bb[:, :], ta[:, :], 1.0, kkn[:, :], ALU.add, ALU.mult)
                elif k in (sD_B0, sD_B1):
                    h = k - sD_B0
                    pD.wait(dve, n, sD_BB)
                    i_ = dve.scalar_tensor_tensor(B_bd[hs(h), :, hs(h)], c8(bb[hs(h), :]), 0.5, c8(Ei[hs(h), :]), ALU.mult, ALU.mult)
                elif k == sD_BV:
                    pP.wait(dve, n, sP_BO)
                    i_ = dve.tensor_tensor(c8(bv[:, q, :]), c8(bank[7]), RAV[:, :, 2, :], ALU.mult)
                pD.inc(i_)

            def chain(s_, c, half):
                n, cb, tg = s_
                if half == 0:
                    uP.wait(dve, n, c + 1)
                    uD.inc(dve.tensor_tensor(U[:, c, :], bank[0][:, c * CH:(c + 1) * CH], Uv[:, c, :], ALU.add))
                else:
                    zP.wait(dve, n, c + 1)
                    if c:
                        zD.wait(dve, n, c)
                    zD.inc(dve.scalar_tensor_tensor(Z[:, cb, (c + 1) % 2, :], Z[:, cb, c % 2, :], E[:, cb % 2, c, CH:CH + 1],
                                                    bank[1][:, c * CH:(c + 1) * CH], ALU.mult, ALU.add))

            def post(s_, k):
                n, cb, tg = s_
                bc = lambda v: v.unsqueeze(2).to_broadcast([P, NC, CH])
                if k == F_SUM:
                    yAll.wait(dve, n, 1)
                    i_ = dve.tensor_reduce(fst[:, 0, :], c8(bank[3]), AX.X, ALU.add)
                elif k == F_NEG:
                    fD.wait(dve, n, F_SUM)
                    i_ = dve.tensor_scalar(fst[:, 0, :], fst[:, 0, :], 1.0 / CH, None, ALU.mult)
                elif k == F_YC:
                    fD.wait(dve, n, F_NEG)
                    i_ = dve.tensor_tensor(c8(yc[:, :]), c8(bank[3]), bc(fst[:, 0, :]), ALU.subtract)
                elif k == F_VAR:
                    fA.wait(dve, n, FA_SQ)
                    i_ = dve.tensor_reduce(fst[:, 1, :], c8(ysq[:, :]), AX.X, ALU.add)
                elif k == F_REC:
                    fA.wait(dve, n, FA_RT)
                    i_ = dve.reciprocal(fst[:, 3, :], fst[:, 2, :])
                elif k == F_YN:
                    fD.wait(dve, n, F_REC)
                    i_ = dve.tensor_tensor(c8(yc[:, :]), c8(yc[:, :]), bc(fst[:, 3, :]), ALU.mult)
                elif k == F_Y2:
                    fA.wait(dve, n, FA_C1)
                    pG.wait(dve, n, sG_BV)
                    i_ = dve.scalar_tensor_tensor(ysb[:, :], ysb[:, :], prm[:, cb, 9:10], bv[:, cb % 2, :], ALU.mult, ALU.add)
                elif k == F_MIX:
                    fD.wait(dve, n, F_Y2)
                    dve.wait_ge(r_out, (n + 1) * 16)
                    i_ = dve.scalar_tensor_tensor(mix[:, :], sg[:, cb % 2, :], 0.5, ysb[:, :], ALU.mult, ALU.mult)
                fD.inc(i_)

            def pair(s_, p_):
                todo = list(range(1, sD_BV + 1)) if p_ else []
                for c in range(NC if s_ else 0):
                    for half in range(2):
                        chain(s_, c, half)
                        if todo:
                            prep(p_, todo.pop(0))
                for k in todo:
                    prep(p_, k)
                if s_:
                    for k in (F_SUM, F_NEG, F_YC):
                        post(s_, k)
                if p_:
                    n = p_[0]
                    for g in range(2):
                        scB.wait(dve, n, g + 1)
                        for h in range(2):
                            i_ = dve.tensor_tensor(SMB[hs(h), gq(g), :, hs(h)], bank[g][hs(h)].rearrange("p (c x t) -> p c x t", c=4, x=2),
                                                   mS[hs(h), :].rearrange("p (x t) -> p x t", x=2).unsqueeze(1).to_broadcast([64, 4, 2, 64]), ALU.mult)
                        smB.inc(i_)
                    wide = lambda m: m.unsqueeze(1).to_broadcast([P, 4, P])
                    for g in range(2):
                        smB.wait(dve, n, g + 1)
                        x0t.link(dve, n, dve.tensor_tensor(XT[:, gq(g), :], SMB[:, gq(g), 1, :], wide(mX1[:, :]), ALU.mult))
                        x0t.inc(dve.tensor_tensor(XT[:, gq(g), :], XT[:, gq(g), :], wide(ident[:, :]), ALU.add))
                    for v in range(NL):
                        for g in range(2):
                            yP.wait(dve, n, 2 * v + g + 1)
                            yD.inc(dve.tensor_tensor(Yl[:, gq(g), :], c4b(g), wide(mL[:, v, :]), ALU.mult))
                        if s_ and v == 0:
                            post(s_, F_VAR)
                        for g in range(2):
                            xP.wait(dve, n, 2 * v + g + 1)
                            dst = X if v < NL - 1 else XT
                            if v < NL - 1:
                                xt_ok.wait(dve, n, 2 * v + g + 1) if v == 0 else xx.wait(dve, n, 2 * v - 1 + g)
                            else:
                                xt_ok.wait(dve, n, 2 * v + g + 1)
                            xx.inc(dve.tensor_tensor(dst[:, gq(g), :], c4b(2 + g), dst[:, gq(g), :], ALU.add))
                        if s_ and v == 0:
                            post(s_, F_REC)
                            post(s_, F_YN)
                        if s_ and v == 2:
                            post(s_, F_Y2)
                            post(s_, F_MIX)
                    for m in (pD, smB, x0t, yD, xx):
                        m.close()
                elif s_:
                    for k in range(F_VAR, F_MIX + 1):
                        post(s_, k)
                if s_:
                    for m in (uD, zD, fD):
                        m.close()
            units(dve, pair)

        def rwkv_tensor(pe, l):
            pe.wait_ge(r_cst, 16 * 7)
            pe.wait_ge(r_once, 4)

            def prep(p_, k):
                n, cb, tg = p_
                if k == sP_ZW:
                    if cb == 0:
                        lA.wait(pe, tg, 2)
                    i_ = pe.matmul(bank[4], lwp[:, cb, 0, :], lin[:, :], start=True, stop=True)
                elif k == sP_ZA:
                    i_ = pe.matmul(bank[5], lwp[:, cb, 1, :], lin[:, :], start=True, stop=True)
                elif k == sP_SS:
                    pG.wait(pe, n, sG_SQ)
                    i_ = pe.matmul(bank[6], ones_b[:, :], kks[:, :], start=True, stop=True)
                elif k == sP_BO:
                    pD.wait(pe, n, sD_RKB)
                    i_ = pe.matmul(bank[7], ones_b[:, :], rkb[:, :], start=True, stop=True)
                pP.inc(i_)

            def chain(s_, c, half):
                n, cb, tg = s_
                col = slice(c * CH, (c + 1) * CH)
                zc = Z[:, cb, c % 2, :]
                if half == 0:
                    if c:
                        zD.wait(pe, n, c)
                    uP.inc(pe.matmul(bank[0][:, col], WT[:, c, :], zc, start=True, stop=True))
                    pe.matmul(bank[1][:, col], Kh_tok[:, c, :], V_tok[:, c, :], start=True, stop=False)
                    pe.matmul(bank[3][:, col], R_bd[:, cb % 2, c, :], zc, start=True, stop=False)
                    pe.matmul(bank[3][:, col], SMK[:, c, 0, :], V_tok[:, c, :], start=False, stop=False)
                else:
                    uD.wait(pe, n, c + 1)
                    zP.inc(pe.matmul(bank[1][:, col], Bh_tok[:, c, :], U[:, c, :], start=False, stop=True))
                    y_ = pe.matmul(bank[3][:, col], SMB[:, c, 0, :], U[:, c, :], start=False, stop=True)
                    if c == NC - 1:
                        yAll.inc(y_)

            def group(g, out, lhs, rhs, first=0):
                for c in range(4 * g, 4 * g + 4):
                    mm = pe.matmul(out[:, (c - 4 * g) * P:(c - 4 * g + 1) * P], lhs(c), rhs(c), start=True, stop=True)
                return mm

            def turn(g, out, src):
                for c in range(4 * g, 4 * g + 4):
                    mm = pe.transpose(out[:, (c - 4 * g) * P:(c - 4 * g + 1) * P], src(c), ident[:, :])
                return mm

            def pair(s_, p_):
                if s_:
                    for c in range(NC):
                        chain(s_, c, 0)
                        if p_ and c in (1, 2, 3):
                            prep(p_, c)
                        if p_ and c == NC - 1:
                            prep(p_, sP_BO)
                        chain(s_, c, 1)
                elif p_:
                    for k in (sP_ZW, sP_ZA, sP_SS, sP_BO):
                        prep(p_, k)

                def out_turn():
                    fD.wait(pe, s_[0], F_YN)
                    if p_:
                        bkE.wait(pe, p_[0], 1)
                    for c in range(NC):
                        mm = pe.transpose(bank[6 + c // 4][0:64, (c % 4) * P:(c % 4 + 1) * P], yc[:, c * CH:(c + 1) * CH], ident[:, :])
                    fP.inc(mm)
                if p_:
                    n = p_[0]
                    pD.wait(pe, n, sD_B1)
                    pG.wait(pe, n, sG_R)
                    for g in range(2):
                        scB.inc(group(g, bank[g], lambda c: B_bd[:, c, :], lambda c: RAV[:, c, 0:2, :]))
                    pG.wait(pe, n, sG_K1)
                    scK.inc(group(0, bank[2], lambda c: K_bd[:, c, :], lambda c: RAV[:, c, 0:2, :]))
                    pA.wait(pe, n, sA_TA)
                    for g in range(2):
                        mm = turn(g, bank[4 + g], lambda c: RAV[:, c, 1:3, :])
                    tAV.inc(mm)
                    for g in range(2):
                        x0t.wait(pe, n, 2 * g + 2)
                        tP.inc(turn(g, bank[g], lambda c: XT[:, c, :]))
                    if s_:
                        fD.wait(pe, s_[0], F_YC)
                    scK.inc(group(1, bank[3], lambda c: K_bd[:, c, :], lambda c: RAV[:, c, 0:2, :]))
                    pG.wait(pe, n, sG_BH)
                    pD.wait(pe, n, sD_BV)
                    for g in range(2):
                        mm = turn(g, bank[6 + g], lambda c: BKh[:, c, :, :])
                    tBK.inc(mm)
                    for v in range(NL):
                        for g in range(2):
                            xt_ok.wait(pe, n, 2 * v + g + 1)
                            yP.inc(group(g, bank[g], lambda c: SMB[:, c, 1, :], lambda c: X[:, c, :]))
                        if v == 0:
                            avE.wait(pe, n, 1)
                            smK.wait(pe, n, 2)
                            for c in range(NC):
                                mm = pe.matmul(bank[4][:, c * CH:(c + 1) * CH], SMK[:, c, 1, :], V_tok[:, c, :], start=True, stop=True)
                            mvP.inc(mm)
                            kcp.wait(pe, n, 2)
                        for g in range(2):
                            yD.wait(pe, n, 2 * v + g + 1)
                            if v < NL - 1:
                                xP.inc(group(g, bank[2 + g], lambda c: XT[:, c, :], lambda c: Yl[:, c, :]))
                            else:
                                xP.inc(group(g, bank[2 + g], lambda c: Yl[:, c, :], lambda c: XT[:, c, :]))
                        if v < NL - 1:
                            for g in range(2):
                                xx.wait(pe, n, 2 * v + g + 1)
                                tP.inc(turn(g, bank[g], lambda c: X[:, c, :]))
                        if v == 0 and s_:
                            out_turn()
                    for g in range(2):
                        xx.wait(pe, n, 2 * NL - 1 + g)
                        mm = group(g, bank[g], lambda c: A_tok[:, c, :], lambda c: XT[:, c, :])
                    wtP.inc(mm)
                    mvA.wait(pe, n, 1)
                    for c in range(NC):
                        mm = pe.matmul(bank[5][:, c * CH:(c + 1) * CH], XT[:, c, :], MV[:, c, :], start=True, stop=True)
                    uvP.inc(mm)
                    wtA.wait(pe, n, 1)
                    uvA.wait(pe, n, 1)
                    for m in (pP, scB, tAV, scK, tBK, yP, xP, mvP, wtP, uvP):
                        m.close()
                    tP.j = 0
                else:
                    out_turn()
                if s_:
                    for m in (uP, zP, yAll, fP):
                        m.close()
            units(pe, pair)

        cv = Carve()
        phase_sems()
        kT, qz, vT, vtok = cv(SEQ), cv(2, SEQ), cv(SEQ), cv(NT, P)
        cg, csg, cmix = cv(SEQ), cv(SEQ), cv(SEQ)
        S = cv(3, 2, SEQ)
        PT_ = cv(2, NT, P)
        O, osq = cv(NT, P), cv(P)
        mxp, nm, l12, cc_, ssq, fs = cv(2, 2, 8), cv(2, 2), cv(NT, 2), cv(2, 2), cv(NT), cv(NT)
        lam, lamv, sub = cv(4, 64), cv(8), cv(4)
        dmask = cv(P)
        c_lv = psem("c_lv")
        c_sems = [c_lv]

        def cmark(name, per, unit=1, credit=0):
            m = Mark(psem("c_" + name), per, unit, credit)
            c_sems.append(m.sem)
            return m
        NB = FIRST[NT]
        c_kq, c_v, c_g = cmark("in_kq", 3, 16), cmark("in_v", 1, 16), cmark("in_gate", 1, 16)
        free_kq, free_v, free_g = cmark("kq_free", 1, credit=1), cmark("v_free", 1, credit=1), cmark("g_free", 1, credit=1)
        c_cst, c_z, c_lam, c_sto = [cmark(n, 1) for n in ("cst", "zero", "lam", "store")]
        vt_ok, ve_ok = cmark("v_turned", 4), cmark("v_out", 4)
        s_ok, se_ok = cmark("scores", NB), cmark("scores_out", NB)
        mx_ok, ex_ok, cb_ok = cmark("max", NT), cmark("exp", NT), cmark("diff", NT)
        pt_ok, pa_ok = cmark("turned", NB), cmark("turned_out", NB)
        pv_ok, o_ok, on_ok = cmark("pv", NT), cmark("o_out", NT), cmark("o_scaled", 4)
        rt_ok, ot_ok, oe_ok = cmark("root", 1), cmark("o_turned", 4), cmark("head", 4, credit=4)
        gt_ok, sg_ok = cmark("gate_tanh", 1), cmark("gate", 1)
        cl = cmark("dve_chain", C_LINKS)

        def attn_sync(sp, l):
            sp.dma_start(dmask[:, :], ins["dmask"]).then_inc(c_cst.sem, 16)
            sp.dma_start(lam[:, :, :], ins["lam"][bass.ds(l, 1)].rearrange("l p a b -> (l p) a b")).then_inc(c_cst.sem, 16)
            sp.dma_start(sub[:, 0:3], ins["sub"][bass.ds(l, 1)].rearrange("l p a -> (l p) a")).then_inc(c_cst.sem, 16)
            c_z.wait(sp, 0, 1)
            with sp.Fori(0, HEADS) as h:
                base = l * COLS + h * P
                def rows(row, n):
                    return PT[bass.ds(base + row, n), 1:SEQ + 1]
                free_v.wait_before(sp, h)
                sp.dma_start(vT[:, :], rows(V_ROW, P)).then_inc(c_v.sem, 16)
                free_kq.wait_before(sp, h)
                for dst, row, n in ((qz[0:64, 0, :], Q_ROW, 64), (qz[64:128, 1, :], Q_ROW + 64, 64), (kT[:, :], K_ROW, P)):
                    sp.dma_start(dst, rows(row, n)).then_inc(c_kq.sem, 16)
                free_g.wait_before(sp, h)
                sp.dma_start(cg[:, :], rows(DG_ROW, P)).then_inc(c_g.sem, 16)

        def attn_scalar(act, l):
            act.wait_ge(c_lam.sem, 1)
            act.activation(lamv[:, 2:4], lamv[:, 0:2], ACT.Exp).then_inc(c_lam.sem, 1)
            with act.Fori(0, HEADS) as h:
                for g in range(4):
                    vt_ok.wait(act, h, g + 1)
                    ve_ok.inc(act.activation(vtok[:, 4 * g:4 * g + 4, :], bank[6 + g % 2].rearrange("p (c t) -> p c t", c=4), ACT.Copy))

                def exp(s_, a):
                    i = ORDER[s_]
                    if a == 0:
                        mx_ok.wait(act, h, s_ + 1)
                    w = (i + 1) * P
                    return act.activation(S[:, s_ % 3, a, 0:w], S[:, s_ % 3, a, 0:w], ACT.Exp, bias=nm[:, s_ % 2, a:a + 1], accum_out=l12[:, i, a:a + 1])
                for s_ in range(NT + 2):
                    exps = [0, 1] if 1 <= s_ <= NT else []
                    nb = BLOCKS[s_ - 2] if s_ >= 2 else 0
                    for j in range(max(nb, 2)):
                        if exps:
                            e = exp(s_ - 1, exps.pop(0))
                            if not exps:
                                ex_ok.inc(e)
                        if j < nb:
                            G, i = FIRST[s_ - 2] + j, ORDER[s_ - 2]
                            pt_ok.wait(act, h, G + 1)
                            w = min(4, i + 1 - 4 * j)
                            pa_ok.inc(act.activation(PT_[:, s_ % 2, 4 * j:4 * j + w, :], bank[4 + G % 2][:, 0:w * P].rearrange("p (c t) -> p c t", t=P), ACT.Copy))
                    if s_ >= 2:
                        i = ORDER[s_ - 2]
                        pv_ok.wait(act, h, s_ - 1)
                        act.activation(O[:, i, :], bank[6 + s_ % 2][:, 0:P], ACT.Copy)
                        o_ok.inc(act.activation(osq[:, :], bank[6 + s_ % 2][:, 0:P], ACT.Square, accum_out=ssq[:, i:i + 1]))
                    if s_ == 3:
                        act.wait_ge(c_g.sem, (h + 1) * 16)
                        gt_ok.inc(act.activation(csg[:, :], cg[:, :], ACT.Tanh, scale=0.5))
                cl.wait(act, h, C_LINKS - 1)
                rt_ok.inc(act.activation(fs[:, :], fs[:, :], ACT.Sqrt))
                oe_ok.wait(act, h, 4)
                act.dma_start(MT[bass.ds(RW + h * P, P), 0:SEQ], cmix[:, :]).then_inc(c_sto.sem, 16)
                for m in (ve_ok, gt_ok, pa_ok, o_ok, ex_ok, rt_ok):
                    m.close()
            act.wait_ge(c_sto.sem, 16 * 5)

        def attn_vector(dve, l):
            for m in (oe_ok, free_kq, free_v, free_g):
                m.grant(dve)
            dve.sem_inc(c_sto.sem, 16)
            dve.memset(qz[64:128, 0, :], 0.0)
            c_z.inc(dve.memset(qz[0:64, 1, :], 0.0))
            dve.wait_ge(c_cst.sem, 48)
            lk = lambda ins_, k: (ins_.then_inc(c_lv, 1), dve.wait_ge(c_lv, k))
            lk(dve.tensor_tensor(lam[:, 0:2, :], lam[:, 0:2, :], lam[:, 2:4, :], ALU.mult), 1)
            dve.tensor_reduce(lamv[:, 0:2], lam[:, 0:2, :], AX.X, ALU.add).then_inc(c_lam.sem, 1)
            dve.wait_ge(c_lam.sem, 2)
            lk(dve.tensor_tensor(lamv[:, 4:5], lamv[:, 3:4], lamv[:, 2:3], ALU.subtract), 2)
            lk(dve.tensor_tensor(lamv[:, 5:6], lamv[:, 4:5], sub[:, 1:2], ALU.subtract), 3)
            lk(dve.tensor_scalar(sub[:, 3:4], sub[:, 0:1], sub[:, 2:3], 0.5, ALU.mult, ALU.mult), 4)
            dve.sem_inc(tick, 1)
            with dve.Fori(0, HEADS) as h:
                def scores_out(s_, j):
                    i, nb, J = ORDER[s_], BLOCKS[s_], FIRST[s_] + j
                    s_ok.wait(dve, h, J + 1)
                    w = GRP if j < nb - 1 else (i % 4) * P
                    for a in range(2):
                        ps_ = bank[2 * (J % 2) + a]
                        if w:
                            x_ = dve.tensor_scalar(S[:, s_ % 3, a, j * GRP:j * GRP + w], ps_[:, 0:w], 0.125, NEG, ALU.mult, ALU.max, accum_out=mxp[:, s_ % 2, a, j:j + 1])
                        if j == nb - 1:
                            x_ = dve.scalar_tensor_tensor(S[:, s_ % 3, a, i * P:(i + 1) * P], ps_[:, w:w + P], 0.125, dmask[:, :], ALU.mult, ALU.add)
                    se_ok.inc(x_)
                for s_ in range(NT + 1):
                    if s_ < NT:
                        i, nb = ORDER[s_], BLOCKS[s_]
                        if s_ > 2:
                            pt_ok.wait(dve, h, FIRST[s_ - 2])
                        for j in range(nb):
                            scores_out(s_, j)
                        n_ = nb if i % 4 else nb - 1
                        se_ok.wait(dve, h, FIRST[s_ + 1])
                        cl.link(dve, h, dve.tensor_reduce(mxp[:, s_ % 2, :, n_:n_ + 1], S[:, s_ % 3, :, i * P:(i + 1) * P], AX.X, ALU.max))
                        cl.link(dve, h, dve.tensor_reduce(nm[:, s_ % 2, :], mxp[:, s_ % 2, :, 0:n_ + 1], AX.X, ALU.max))
                        mx_ok.inc(dve.tensor_scalar(nm[:, s_ % 2, :], nm[:, s_ % 2, :], -1.0, None, ALU.mult))
                    if s_ == 5:
                        gt_ok.wait(dve, h, 1)
                        sg_ok.link(dve, h, dve.scalar_tensor_tensor(csg[:, :], csg[:, :], 1.0, cg[:, :], ALU.add, ALU.mult))
                        dve.sem_inc(free_g.sem, 1)
                    if s_:
                        t_, i = s_ - 1, ORDER[s_ - 1]
                        w = (i + 1) * P
                        ex_ok.wait(dve, h, s_)
                        cl.link(dve, h, dve.reciprocal(cc_[:, t_ % 2, 0:1], l12[:, i, 1:2]))
                        cl.link(dve, h, dve.tensor_scalar(cc_[:, t_ % 2, 1:2], cc_[:, t_ % 2, 0:1], l12[:, i, 0:1], lamv[:, 5:6], ALU.mult, ALU.mult))
                        cb_ok.inc(dve.scalar_tensor_tensor(S[:, t_ % 3, 0, 0:w], S[:, t_ % 3, 1, 0:w], cc_[:, t_ % 2, 1:2], S[:, t_ % 3, 0, 0:w], ALU.mult, ALU.add))
                cl.link(dve, h, dve.tensor_tensor(fs[:, :], l12[:, :, 0], l12[:, :, 0], ALU.mult))
                cl.link(dve, h, dve.tensor_scalar(fs[:, :], fs[:, :], SUBLN_EPS * P, None, ALU.mult))
                o_ok.wait(dve, h, NT)
                cl.link(dve, h, dve.tensor_tensor(fs[:, :], fs[:, :], ssq[:, :], ALU.add))
                cl.link(dve, h, dve.tensor_scalar(fs[:, :], fs[:, :], 1.0 / P, None, ALU.mult))
                rt_ok.wait(dve, h, 1)
                cl.link(dve, h, dve.reciprocal(fs[:, :], fs[:, :]))
                for g in range(4):
                    on_ok.inc(dve.tensor_tensor(O[:, 4 * g:4 * g + 4, :], O[:, 4 * g:4 * g + 4, :], fs[:, 4 * g:4 * g + 4].unsqueeze(2).to_broadcast([P, 4, P]), ALU.mult))
                dve.wait_ge(c_sto.sem, (h + 1) * 16)
                for g in range(4):
                    ot_ok.wait(dve, h, g + 1)
                    oe_ok.inc(dve.scalar_tensor_tensor(cmix[:, g * GRP:(g + 1) * GRP], bank[4 + g % 2], sub[:, 3:4], csg[:, g * GRP:(g + 1) * GRP], ALU.mult, ALU.mult))
                for m in (se_ok, mx_ok, cb_ok, on_ok, sg_ok, oe_ok, cl):
                    m.close()

        def attn_tensor(pe, l):
            with pe.Fori(0, HEADS) as h:
                def scores(s_, j):
                    i, J = ORDER[s_], FIRST[s_] + j
                    w = min(GRP, (i + 1) * P - j * GRP)
                    if J >= 2:
                        se_ok.wait(pe, h, J - 1)
                    for a in range(2):
                        mm = pe.matmul(bank[2 * (J % 2) + a][:, 0:w], qz[:, a, i * P:(i + 1) * P], kT[:, j * GRP:j * GRP + w], start=True, stop=True)
                    s_ok.inc(mm)

                def turn_map(s_, j):
                    i, G = ORDER[s_], FIRST[s_] + j
                    if j == 0:
                        cb_ok.wait(pe, h, s_ + 1)
                    if G >= 2:
                        pa_ok.wait(pe, h, G - 1)
                    for c in range(min(4, i + 1 - 4 * j)):
                        k = 4 * j + c
                        mm = pe.transpose(bank[4 + G % 2][:, c * P:(c + 1) * P], S[:, s_ % 3, 0, k * P:(k + 1) * P], ident[:, :])
                    pt_ok.inc(mm)

                def values(s_, j):
                    i, G = ORDER[s_], FIRST[s_] + j
                    if j == 0 and s_ > 1:
                        o_ok.wait(pe, h, s_ - 1)
                    pa_ok.wait(pe, h, G + 1)
                    for c in range(min(4, i + 1 - 4 * j)):
                        k = 4 * j + c
                        mm = pe.matmul(bank[6 + s_ % 2][:, 0:P], PT_[:, s_ % 2, k, :], vtok[:, k, :], start=(k == 0), stop=(k == i))
                    if j == BLOCKS[s_] - 1:
                        pv_ok.inc(mm)
                c_v.wait(pe, h, 1)
                for g in range(4):
                    if g > 1:
                        ve_ok.wait(pe, h, g - 1)
                    for c in range(4):
                        mm = pe.transpose(bank[6 + g % 2][:, c * P:(c + 1) * P], vT[:, (4 * g + c) * P:(4 * g + c + 1) * P], ident[:, :])
                    vt_ok.inc(mm)
                vt_ok.wait(pe, h, 4)
                pe.sem_inc(free_v.sem, 1)
                c_kq.wait(pe, h, 3)
                for s_ in range(NT + 2):
                    new, old = (BLOCKS[s_] if s_ < NT else 0), (BLOCKS[s_ - 2] if s_ >= 2 else 0)
                    if s_ == 2:
                        ve_ok.wait(pe, h, 4)
                    for j in range(max(new, old + 2)):
                        if j < new:
                            scores(s_, j)
                        if 1 <= j <= old:
                            turn_map(s_ - 2, j - 1)
                        if 2 <= j <= old + 1:
                            values(s_ - 2, j - 2)
                    if s_ == NT - 1:
                        s_ok.wait(pe, h, NB)
                        pe.sem_inc(free_kq.sem, 1)
                for g in range(4):
                    on_ok.wait(pe, h, g + 1)
                    if g > 1:
                        oe_ok.wait(pe, h, g - 1)
                    for c in range(4):
                        mm = pe.transpose(bank[4 + g % 2][:, c * P:(c + 1) * P], O[:, 4 * g + c, :], ident[:, :])
                    ot_ok.inc(mm)
                for m in (vt_ok, s_ok, pt_ok, pv_ok, ot_ok):
                    m.close()

        cv = Carve()
        phase_sems()
        cv.at = ARENA - (KT + 1) * D
        wo, fw = cv(KT, D), cv(D)
        cv.at = 0
        mt = [cv(KT, P) for _ in range(2)]
        xo, yo, osq2, ost2 = cv(2, D), cv(2, D), cv(D), cv(8)
        d_cst = sem("d_cst")
        d_mt, d_xs, d_ys = [psem("d_mt0"), psem("d_mt1")], [psem("d_xs0"), psem("d_xs1")], [psem("d_ys0"), psem("d_ys1")]
        d_mm, d_res, d_ssq, d_rt, d_rc, d_y = [psem("d_" + n) for n in ("mm", "res", "ssq", "rt", "rc", "y")]
        d_sems = [d_cst, d_mm, d_res, d_ssq, d_rt, d_rc, d_y] + d_mt + d_xs + d_ys

        def dslice(t, n):
            return slice(t * P, t * P + n) if isinstance(t, int) else bass.ds(t * P, n)

        def each_tile(eng, tile):
            with eng.Fori(0, NT // 2) as i:
                for u in range(2):
                    tile(i, i * 2 + u, u, P)
            tile(NT // 2, NT, 0, NS)

        def out_sync(sp, l):
            def tile(i, t, u, n):
                sp.wait_ge(d_y, t + 1)
                sp.dma_start(mt[u][:, :, 0:n], MT[:, dslice(t, n)].rearrange("(k p) t -> p k t", p=P)).then_inc(d_mt[u], 16)
                sp.wait_ge(d_xs[u], (i + 1) * 16)
                sp.dma_start(xo[0:n, u, :], xcur[dslice(t, n), :]).then_inc(d_mt[u], 16)
            each_tile(sp, tile)

        def out_scalar(act, l):
            for s_ in d_xs + d_ys:
                act.sem_inc(s_, 16)

            def tile(i, t, u, n):
                act.wait_ge(d_res, t + 1)
                act.dma_start(xcur[dslice(t, n), :], xo[0:n, u, :]).then_inc(d_xs[u], 16)
                act.activation(osq2[0:n, :], xo[0:n, u, :], ACT.Square, accum_out=ost2[0:n, u:u + 1]).then_inc(d_ssq, 1)
                act.wait_ge(d_ssq, t + 1)
                act.activation(ost2[0:n, 2 + u:3 + u], ost2[0:n, u:u + 1], ACT.Sqrt, bias=eps_rms[0:n, :], scale=1.0 / D).then_inc(d_rt, 1)
                act.wait_ge(d_y, t + 3)
                act.dma_start(outs["y"][dslice(t, n), :], yo[0:n, u, :]).then_inc(d_ys[u], 16)
            each_tile(act, tile)
            for u in range(2):
                act.wait_ge(d_xs[u], 16 * (NT // 2 + 2 - u))
                act.wait_ge(d_ys[u], 16 * (NT // 2 + 2 - u))

        def out_vector(dve, l):
            dve.sem_inc(d_y, 2)
            dve.wait_ge(d_cst, 32)

            def tile(i, t, u, n):
                dve.wait_ge(d_mt[u], (i + 1) * 32)
                dve.wait_ge(d_mm, t + 1)
                for q in range(2):
                    r_ = dve.tensor_tensor(xo[0:n, u, q * GRP:(q + 1) * GRP], bank[2 * u + q][0:n, :], xo[0:n, u, q * GRP:(q + 1) * GRP], ALU.add)
                r_.then_inc(d_res, 1)
                dve.wait_ge(d_rt, t + 1)
                dve.reciprocal(ost2[0:n, 4 + u:5 + u], ost2[0:n, 2 + u:3 + u]).then_inc(d_rc, 1)
                dve.wait_ge(d_rc, t + 1)
                dve.wait_ge(d_ys[u], (i + 1) * 16)
                dve.scalar_tensor_tensor(yo[0:n, u, :], xo[0:n, u, :], ost2[0:n, 4 + u:5 + u], fw[0:n, :], ALU.mult, ALU.mult).then_inc(d_y, 1)
            each_tile(dve, tile)

        def out_tensor(pe, l):
            pe.wait_ge(d_cst, 32)

            def tile(i, t, u, n):
                pe.wait_ge(d_mt[u], (i + 1) * 32)
                pe.wait_ge(d_y, t + 1)
                for q in range(2):
                    for k in range(KT):
                        mm = pe.matmul(bank[2 * u + q][0:n, :], mt[u][:, k, 0:n], wo[:, k, q * GRP:(q + 1) * GRP], start=(k == 0), stop=(k == KT - 1))
                mm.then_inc(d_mm, 1)
            each_tile(pe, tile)


        cv = Carve()
        phase_sems()
        W4 = (4, NS)
        t_raw, t_prev, t_mu, t_dif = cv(13, NS), cv(13, 8), cv(13), cv(13, NS)
        t_prm, t_lw, t_gate = cv(4, 16), cv(4, P), cv(*W4)
        t_tw, t_zw, t_ta, t_L, t_Ei = cv(NS), cv(*W4), cv(*W4), cv(P), cv(*W4)
        t_E = cv(4, 8, 5)
        t_kkr, t_sq, t_rn, t_kf, t_bb, t_rkb, t_bv, t_t1 = [cv(*W4) for _ in range(8)]
        t_RAV, t_BK, t_BKh = cv(4, 3, NS), cv(4, 2, NS), cv(4, 2, NS)
        t_AVt, t_BKt = cv(4, P), cv(4, P)
        t_SM, t_X, t_XT, t_Y = cv(2, 4, 64), cv(2, 4, NS), cv(2, 4, NS), cv(2, 4, NS)
        t_MV, t_WR, t_UT = cv(8, 64), cv(4, 8, 8), cv(4, NS)
        t_Z, t_Zn, t_UVm = cv(4, 8, 64), cv(4, 8, 64), cv(8, 8, 64)
        t_y, t_yc, t_ys, t_rs, t_sg, t_mix = [cv(*W4) for _ in range(6)]
        t_mS, t_mR, t_mX, t_eye, t_bm = cv(64), cv(P), cv(3, NS), cv(NS), cv(8)
        t_ones, t_mean = cv(P), cv(P)
        t_in, t_sto = psem("t_in"), psem("t_store")
        t_a, t_d, t_p, t_g = psem("t_scalar_steps"), psem("t_vector_steps"), psem("t_tensor_steps"), psem("t_gpsimd_steps")
        t_sems = [t_in, t_sto, t_a, t_d, t_p, t_g]
        T_IN = 16 * 17
        bcast = lambda v, n: v.unsqueeze(2).to_broadcast([P, v.shape[1], n])
        grp = lambda v: v.rearrange("p c (b t) -> p (c b) t", t=4)
        A_TW, A_ZW, A_ZA, A_NRM, A_E, A_EI, A_GT, A_AV, A_BK, A_MV, A_WT, A_UT, A_U, A_Y, A_SQ, A_RS = range(1, 17)
        P_Z, P_SS, P_BO, P_AV, P_SC, P_MAB, P_BK, P_MV, P_Y, P_XT, P_WT, P_UT, P_U, P_YD, P_ZN, P_MU, P_VAR = range(1, 18)

        def rsmp_sync(sp, l):
            lo_ = l * COLS
            for dst, src in ((t_raw[:, :, :], PT[bass.ds(lo_, 13 * P), SEQ + 1:].rearrange("(j p) t -> p j t", p=P)),
                             (t_prev[:, :, :], ins["prev"][bass.ds(l, 1)].rearrange("l p j b -> (l p) j b")),
                             (t_mu[:, :], ins["mu13"][bass.ds(l, 1)].rearrange("l p j -> (l p) j")),
                             (t_gate[:, :, :], PT[bass.ds(lo_ + GATE_ROW, RW), SEQ + 1:].rearrange("(j p) t -> p j t", p=P)),
                             (t_prm[:, :, :], ins["prm"][bass.ds(l * 4, 4)].rearrange("c p k -> p c k")),
                             (t_lw[:, :, :], ins["lora"][bass.ds(l * 4, 4)].rearrange("c p k -> p c k")),
                             (t_Z[:, :, :, :], ins["z0"][bass.ds(l, 1)].rearrange("l p c b v -> (l p) c b v")),
                             (t_mS[0:64], ins["tmS"]), (t_mR[:, :], ins["tmR"]), (t_mX[0:NS], ins["tmX"]), (t_eye[0:NS, :], ins["eye"][0:NS, 0:NS]),
                             (t_bm[0:64], ins["tbm"]), (t_ones[:, :], ins["ones_b"]), (t_mean[:, :], ins["mean_b"])):
                sp.dma_start(dst, src).then_inc(t_in, 16)

        def rsmp_scalar(act, l):
            N_IN = 16 * 14
            act.wait_ge(t_in, N_IN)
            act.wait_ge(t_d, 4)
            act.activation(t_tw[0:64, :], t_dif[0:64, 12, :], ACT.Tanh).then_inc(t_a, 1)
            act.wait_ge(t_d, 5)
            act.activation(t_zw[:, :, :], t_zw[:, :, :], ACT.Tanh, scale=0.5).then_inc(t_a, 1)
            act.wait_ge(t_d, 6)
            act.activation(t_ta[:, :, :], t_ta[:, :, :], ACT.Tanh, scale=0.5).then_inc(t_a, 1)
            act.wait_ge(t_p, P_SS)
            act.activation(t_rn[:, :, :], bank[2][:, 0:P].rearrange("p (c t) -> p c t", c=4), ACT.Sqrt).then_inc(t_a, 1)
            act.wait_ge(t_d, 8)
            act.activation(t_E[:, :, :, 1:5].rearrange("p c b t -> p (c b) t"), t_L[:, :].rearrange("p (g t) -> p g t", t=4), ACT.Exp).then_inc(t_a, 1)
            act.activation(t_Ei[:, :, :], t_L[:, :].rearrange("p (c t) -> p c t", c=4), ACT.Exp, scale=-1.0).then_inc(t_a, 1)
            act.activation(t_sg[:, :, :], t_gate[:, :, :], ACT.Tanh, scale=0.5).then_inc(t_a, 1)
            act.wait_ge(t_p, P_AV)
            act.activation(t_AVt[0:64, :, :], bank[4][0:64].rearrange("p (c t) -> p c t", c=4), ACT.Copy).then_inc(t_a, 1)
            act.wait_ge(t_p, P_BK)
            act.activation(t_BKt[0:64, :, :], bank[7][0:64].rearrange("p (c t) -> p c t", c=4), ACT.Copy).then_inc(t_a, 1)
            act.wait_ge(t_p, P_MV)
            act.activation(t_MV[0:NS, :, :], bank[0][0:NS].rearrange("p (c t) -> p c t", c=8), ACT.Copy).then_inc(t_a, 1)
            act.wait_ge(t_p, P_WT)
            act.activation(t_WR[:, :, :, 0:4].rearrange("p c b t -> p (c b) t"), bank[1][:, 0:P].rearrange("p (g t) -> p g t", t=4), ACT.Copy).then_inc(t_a, 1)
            act.wait_ge(t_p, P_UT)
            act.activation(grp(t_UT[:, :, :]), bank[2][:, 0:256].rearrange("p (g t) -> p g t", t=8)[:, :, 0:4], ACT.Copy).then_inc(t_a, 1)
            act.wait_ge(t_p, P_U)
            act.activation(t_AVt[0:NS, :, :], bank[3][0:NS].rearrange("p (c t) -> p c t", c=4), ACT.Copy).then_inc(t_a, 1)
            act.wait_ge(t_p, P_YD)
            act.activation(grp(t_y[:, :, :]), bank[2][:, 0:256].rearrange("p (g t) -> p g t", t=8)[:, :, 4:8], ACT.Copy).then_inc(t_a, 1)
            act.wait_ge(t_d, T_YC)
            act.activation(t_ys[:, :, :], t_yc[:, :, :], ACT.Square).then_inc(t_a, 1)
            act.wait_ge(t_p, P_VAR)
            act.activation(t_rs[:, :, :], bank[1][:, 0:P].rearrange("p (c t) -> p c t", c=4), ACT.Sqrt, bias=eps_gn[:, :]).then_inc(t_a, 1)
            act.wait_ge(t_d, T_ZN)
            act.dma_start(outs["ss"][bass.ds(l * RW, RW)].rearrange("(c p) b v -> p c b v", p=P), t_Zn[:, :, :, :]).then_inc(t_sto, 16)
            act.wait_ge(t_d, T_END)
            act.dma_start(MT[0:RW, SEQ:TOK].rearrange("(c p) t -> p c t", p=P), t_mix[:, :, :]).then_inc(t_sto, 16)
            act.wait_ge(t_sto, 32)

        T_YC, T_ZN, T_END = 37, 36, 46

        def rsmp_vector(dve, l):
            k = [0]

            def step(ins_, hold=True):
                k[0] += 1
                ins_.then_inc(t_d, 1)
                if hold:
                    dve.wait_ge(t_d, k[0])
                return k[0]
            pc = lambda c: bcast(t_prm[:, :, c], NS)
            f4 = lambda v: v.rearrange("p (c t) -> p c t", c=4)
            dve.wait_ge(t_in, 16 * 14)
            gr = t_raw[:, :, :].rearrange("p j (b t) -> p (j b) t", t=4)
            gd = t_dif[:, :, :].rearrange("p j (b t) -> p (j b) t", t=4)
            step(dve.tensor_tensor(gd[:, :, 0], t_prev[:, :, :].rearrange("p j b -> p (j b)"), gr[:, :, 0], ALU.subtract), False)
            step(dve.tensor_tensor(gd[:, :, 1:4], gr[:, :, 0:3], gr[:, :, 1:4], ALU.subtract))
            step(dve.tensor_tensor(t_dif[:, :, :], t_dif[:, :, :], bcast(t_mu[:, :], NS), ALU.mult))
            step(dve.tensor_tensor(t_dif[:, :, :], t_dif[:, :, :], t_raw[:, :, :], ALU.add))
            r_, k_, v_ = t_dif[:, 0:4, :], t_dif[:, 4:8, :], t_dif[:, 8:12, :]
            dve.wait_ge(t_p, P_Z)
            step(dve.tensor_tensor(t_zw[:, :, :], f4(bank[0][:, 0:P]), pc(4), ALU.add), False)
            step(dve.tensor_tensor(t_ta[:, :, :], f4(bank[1][:, 0:P]), pc(5), ALU.add), False)
            dve.wait_ge(t_a, A_ZW)
            step(dve.tensor_scalar(t_zw[:, :, :], t_zw[:, :, :], 1.0, -0.5 * DECAY, ALU.add, ALU.mult))
            step(dve.tensor_tensor_scan(t_L[:, :], t_mR[:, :], t_zw[:, :, :].rearrange("p c t -> p (c t)"), 0.0, ALU.mult, ALU.add), False)
            dve.wait_ge(t_a, A_ZA)
            step(dve.tensor_scalar(t_t1[:, :, :], t_ta[:, :, :], 1.0, 0.5, ALU.subtract, ALU.mult))
            step(dve.tensor_tensor(t_t1[:, :, :], t_t1[:, :, :], pc(7), ALU.mult))
            step(dve.scalar_tensor_tensor(t_kf[:, :, :], t_t1[:, :, :], 1.0, k_, ALU.add, ALU.mult))
            step(dve.tensor_tensor(t_rkb[:, :, :], r_, t_kf[:, :, :], ALU.mult))
            step(dve.tensor_tensor(t_rkb[:, :, :], t_rkb[:, :, :], pc(8), ALU.mult), False)
            dve.wait_ge(t_a, A_EI)
            c4 = lambda v: v.rearrange("p c (b t) -> p c b t", t=4)
            step(dve.tensor_tensor(c4(t_RAV[:, :, 0, :]), c4(r_), t_E[:, :, :, 1:5], ALU.mult))
            step(dve.tensor_tensor(t_BK[:, :, 1, :], t_kf[:, :, :], t_Ei[:, :, :], ALU.mult), False)
            step(dve.tensor_copy(t_RAV[:, :, 2, :], v_), False)
            step(dve.tensor_copy(t_WR[:, :, :, 4:8], c4(t_RAV[:, :, 0, :])), False)
            step(dve.tensor_scalar(t_rn[:, :, :], t_rn[:, :, :], 1e-12, None, ALU.max))
            step(dve.reciprocal(t_rn[:, :, :], t_rn[:, :, :]))
            dve.wait_ge(t_g, 1)
            step(dve.tensor_tensor(t_rn[:, :, :], t_kkr[:, :, :], t_rn[:, :, :], ALU.mult))
            step(dve.scalar_tensor_tensor(t_bb[:, :, :], t_ta[:, :, :], 1.0, t_rn[:, :, :], ALU.add, ALU.mult), False)
            step(dve.tensor_scalar(t_rn[:, :, :], t_rn[:, :, :], -1.0, None, ALU.mult))
            step(dve.tensor_tensor(c4(t_RAV[:, :, 1, :]), c4(t_rn[:, :, :]), t_E[:, :, :, 0:4], ALU.mult), False)
            step(dve.scalar_tensor_tensor(t_BK[:, :, 0, :], t_bb[:, :, :], 0.5, t_Ei[:, :, :], ALU.mult, ALU.mult), False)
            dve.wait_ge(t_p, P_BO)
            step(dve.tensor_tensor(t_bv[:, :, :], f4(bank[3][:, 0:P]), t_RAV[:, :, 2, :], ALU.mult), False)
            bc3 = lambda m, n: m.unsqueeze(1).to_broadcast([m.shape[0], 2, n]).unsqueeze(2).to_broadcast([m.shape[0], 2, 4, n])
            dve.wait_ge(t_p, P_SC)
            step(dve.tensor_tensor(t_SM[0:64], psum[0:64, 5:7, 0:256].rearrange("p h (c t) -> p h c t", c=4), bc3(t_mS[0:64, :], 64), ALU.mult), False)
            dve.wait_ge(t_p, P_MAB)
            step(dve.tensor_tensor(t_X[0:NS], psum[0:NS, 2:4, 0:P].rearrange("p h (c t) -> p h c t", c=4), bc3(t_mX[0:NS, 0, :], NS), ALU.mult))
            step(dve.tensor_tensor(t_X[0:NS], t_X[0:NS], bc3(t_eye[0:NS, :], NS), ALU.add), False)
            step(dve.tensor_tensor(t_XT[0:NS], t_SM[0:NS, :, :, NS:64], bc3(t_mX[0:NS, 1, :], NS), ALU.mult))
            step(dve.tensor_tensor(t_XT[0:NS], t_XT[0:NS], bc3(t_eye[0:NS, :], NS), ALU.add), False)
            dve.wait_ge(t_p, P_Y)
            step(dve.tensor_tensor(t_Y[0:NS], bank[4][0:NS, 0:256].rearrange("p (h c t) -> p h c t", h=2, c=4), bc3(t_mX[0:NS, 2, :], NS), ALU.mult), False)
            dve.wait_ge(t_p, P_XT)
            step(dve.tensor_tensor(t_XT[0:NS], bank[5][0:NS, 0:256].rearrange("p (h c t) -> p h c t", h=2, c=4), t_XT[0:NS], ALU.add), False)
            dve.wait_ge(t_a, A_U)
            step(dve.tensor_tensor(t_UVm[0:64], t_AVt[0:64, :, :].rearrange("p c (h v) -> p (c h) v", h=2).unsqueeze(2).to_broadcast([64, 8, 8, 64]),
                                   t_bm[0:64, :].unsqueeze(1).to_broadcast([64, 8, 8]).unsqueeze(3).to_broadcast([64, 8, 8, 64]), ALU.mult), False)
            dve.wait_ge(t_p, P_MU)
            step(dve.tensor_tensor(t_Zn[:, :, :, :].rearrange("p c b v -> p (c b) v"), t_Z[:, :, :, :].rearrange("p c b v -> p (c b) v"),
                                   t_E[:, :, :, 4:5].rearrange("p c b t -> p (c b) t").to_broadcast([P, 32, 64]), ALU.mult))
            step(dve.tensor_copy(t_t1[:, 0, 0:1], t_t1[:, 0, 0:1]))
            step(dve.tensor_tensor(t_Zn[:, :, :, :].rearrange("p c b v -> p c (b v)"), psum[:, 4:8, :], t_Zn[:, :, :, :].rearrange("p c b v -> p c (b v)"), ALU.add), False)
            step(dve.tensor_tensor(t_yc[:, :, :], t_y[:, :, :], f4(bank[0][:, 0:P]), ALU.subtract), False)
            dve.wait_ge(t_a, A_RS)
            step(dve.reciprocal(t_rs[:, :, :], t_rs[:, :, :]))
            step(dve.tensor_tensor(t_yc[:, :, :], t_yc[:, :, :], t_rs[:, :, :], ALU.mult))
            step(dve.tensor_tensor(t_yc[:, :, :], t_yc[:, :, :], pc(9), ALU.mult))
            step(dve.tensor_tensor(t_yc[:, :, :], t_yc[:, :, :], pc(10), ALU.add))
            step(dve.tensor_tensor(t_yc[:, :, :], t_yc[:, :, :], t_bv[:, :, :], ALU.add))
            step(dve.scalar_tensor_tensor(t_sg[:, :, :], t_sg[:, :, :], 1.0, t_gate[:, :, :], ALU.add, ALU.mult))
            step(dve.tensor_scalar(t_sg[:, :, :], t_sg[:, :, :], 0.5, None, ALU.mult))
            step(dve.tensor_tensor(t_mix[:, :, :], t_sg[:, :, :], t_yc[:, :, :], ALU.mult), False)
            step(dve.tensor_copy(t_t1[:, 0, 0:1], t_t1[:, 0, 0:1]), False)
            assert k[0] == T_END, k

        def rsmp_gpsimd(pool, l):
            pool.wait_ge(t_in, 16 * 14)
            pool.memset(t_E[:, :, :, 0:1], 1.0)
            pool.wait_ge(t_d, 4)
            pool.tensor_tensor(t_kkr[:, :, :], t_dif[:, 4:8, :], bcast(t_prm[:, :, 6], NS), ALU.mult).then_inc(t_g, 1)
            pool.wait_ge(t_g, 1)
            pool.tensor_tensor(t_sq[:, :, :], t_kkr[:, :, :], t_kkr[:, :, :], ALU.mult).then_inc(t_g, 1)
            pool.wait_ge(t_d, 24)
            for a in range(2):
                g_ = pool.tensor_tensor(t_BKh[:, :, a, :].rearrange("p c (b t) -> p c b t", t=4), t_BK[:, :, a, :].rearrange("p c (b t) -> p c b t", t=4),
                                        t_E[:, :, :, 4:5].to_broadcast([P, 4, 8, 4]), ALU.mult)
            g_.then_inc(t_g, 1)

        def rsmp_tensor(pe, l):
            hs = lambda h: slice(64 * h, 64 * h + 64)
            pe.wait_ge(t_in, 16 * 14)
            pe.wait_ge(t_a, A_TW)
            for c in range(4):
                pe.matmul(bank[0][:, c * NS:(c + 1) * NS], t_lw[0:64, c, :], t_tw[0:64, :], start=True, stop=True)
            for c in range(4):
                mm = pe.matmul(bank[1][:, c * NS:(c + 1) * NS], t_lw[64:128, c, :], t_dif[64:128, 12, :], start=True, stop=True)
            mm.then_inc(t_p, 1)
            pe.wait_ge(t_g, 2)
            pe.matmul(bank[2][:, 0:P], t_ones[:, :], t_sq[:, :, :], start=True, stop=True).then_inc(t_p, 1)
            pe.wait_ge(t_d, 13)
            pe.matmul(bank[3][:, 0:P], t_ones[:, :], t_rkb[:, :, :], start=True, stop=True).then_inc(t_p, 1)
            pe.wait_ge(t_d, 24)
            for c in range(4):
                mm = pe.transpose(bank[4][0:64, c * P:(c + 1) * P], t_RAV[:, c, 1:3, :], ident[:, :])
            mm.then_inc(t_p, 1)
            for h in range(2):
                for c in range(4):
                    mm = pe.matmul(bank[5 + h][0:64, c * 64:(c + 1) * 64], t_BK[hs(h), c, :, :], t_RAV[hs(h), c, 0:2, :], start=True, stop=True)
            mm.then_inc(t_p, 1)
            pe.wait_ge(t_d, 25)
            pe.wait_ge(t_a, A_NRM)
            for h in range(2):
                for c in range(4):
                    mm = pe.matmul(bank[2 + h][0:NS, c * NS:(c + 1) * NS], t_RAV[hs(h), c, 1, :], t_BK[hs(h), c, 0, :], start=True, stop=True)
            mm.then_inc(t_p, 1)
            pe.wait_ge(t_g, 3)
            for c in range(4):
                mm = pe.transpose(bank[7][0:64, c * P:(c + 1) * P], t_BKh[:, c, :, :], ident[:, :])
            mm.then_inc(t_p, 1)
            pe.wait_ge(t_d, 26)
            pe.wait_ge(t_a, A_AV)
            for h in range(2):
                for c in range(4):
                    u = h * 4 + c
                    mm = pe.matmul(bank[0][0:NS, u * 64:(u + 1) * 64], t_SM[NS:64, h, c, NS:64], t_AVt[NS:64, c, hs(h)], start=True, stop=True)
            mm.then_inc(t_p, 1)
            pe.wait_ge(t_d, 30)
            for h in range(2):
                for c in range(4):
                    u = h * 4 + c
                    mm = pe.matmul(bank[4][0:NS, u * NS:(u + 1) * NS], t_SM[0:NS, h, c, NS:64], t_X[0:NS, h, c, :], start=True, stop=True)
            mm.then_inc(t_p, 1)
            pe.wait_ge(t_d, 31)
            for h in range(2):
                for c in range(4):
                    u = h * 4 + c
                    mm = pe.matmul(bank[5][0:NS, u * NS:(u + 1) * NS], t_Y[0:NS, h, c, :], t_XT[0:NS, h, c, :], start=True, stop=True)
            mm.then_inc(t_p, 1)
            pe.wait_ge(t_d, 32)
            for h in range(2):
                for c in range(4):
                    mm = pe.matmul(bank[1][hs(h), c * NS:(c + 1) * NS], t_AVt[0:NS, c, hs(h)], t_XT[0:NS, h, c, :], start=True, stop=True)
            mm.then_inc(t_p, 1)
            pe.wait_ge(t_a, A_WT)
            u8 = bank[2][:, 0:256].rearrange("p (c b t) -> p c b t", c=4, b=8)
            for h in range(2):
                for c in range(4):
                    pe.matmul(u8[hs(h), c, :, 0:4], t_MV[0:NS, h * 4 + c, :], t_XT[0:NS, h, c, :], start=(c == 0), stop=False, skip_group_check=True)
            for h in range(2):
                for c in range(4):
                    for b in range(8):
                        mm = pe.matmul(u8[hs(h), c, b, :], t_Z[hs(h), c, b, :], t_WR[hs(h), c, b, :], start=False, stop=False, skip_group_check=True)
            mm.then_inc(t_p, 1)
            pe.wait_ge(t_a, A_UT)
            for c in range(4):
                mm = pe.transpose(bank[3][0:NS, c * P:(c + 1) * P], t_UT[:, c, :], ident[:, :])
            mm.then_inc(t_p, 1)
            pe.wait_ge(t_a, A_U)
            for h in range(2):
                for c in range(4):
                    mm = pe.matmul(u8[hs(h), c, :, 4:8], t_AVt[0:64, c, hs(h)], t_SM[0:64, h, c, 0:NS], start=False, stop=True, skip_group_check=True)
            mm.then_inc(t_p, 1)
            pe.wait_ge(t_d, 33)
            for c in range(4):
                for h in range(2):
                    mm = pe.matmul(bank[4 + c][hs(h), :], t_BKt[0:64, c, hs(h)], t_UVm[0:64, 2 * c + h, :, :], start=True, stop=True)
            mm.then_inc(t_p, 1)
            pe.wait_ge(t_a, A_Y)
            pe.matmul(bank[0][:, 0:P], t_mean[:, :], t_y[:, :, :], start=True, stop=True).then_inc(t_p, 1)
            pe.wait_ge(t_a, A_SQ)
            pe.matmul(bank[1][:, 0:P], t_mean[:, :], t_ys[:, :, :], start=True, stop=True).then_inc(t_p, 1)

        cv = Carve()
        phase_sems()
        PG, NP, KS = 128, SEQ // 128, 8
        kpg, vpg, kTs = cv(KS, 512), cv(NP, 512), cv(2, 4, 512)
        ptab = sb("ptab", [1, 8 * NP], I32)
        qT_s, kT_s, vT_s, g_s, sg_s = [cv(4, NS) for _ in range(5)]
        Qs, qb, vt_s = cv(4, 8, NS), cv(4, NS), cv(512)
        Pq, Pn, PTs, PTn = cv(SEQ), cv(NS), cv(NP, NS), cv(NS)
        n_m, u_st, u_cs, fold = cv(8, NS), cv(16), cv(2), cv(16)
        Ob, O_s, osq_s, ors, omx = cv(512), cv(4, NS), cv(4, NS), cv(4, NS), cv(4, NS)
        onesP, u_lam, u_lamv, u_sub = cv(P), cv(4, 64), cv(8), cv(4)
        u_sems = []

        def umark(name, per, unit=1, credit=0):
            m = Mark(psem("u_" + name), per, unit, credit)
            u_sems.append(m.sem)
            return m
        u_k = [umark(f"k{i}", 2, 16) for i in range(KS)]
        u_v = umark("v", NP, 16)
        u_in, u_lv, u_q, u_pp, u_pa = [umark(n, 1) for n in ("in", "lam", "queries", "pe_once", "act_once")]
        kt_ok, kea, ked = umark("k_turned", NP, credit=KS), umark("k_out_act", NP // 2, credit=1), umark("k_out_dve", NP // 2, credit=1)
        qb_ok, sc2, scn = umark("qb", 1), umark("scores", 4), umark("scores_new", 1)
        n_ok, m_ok, e2_ok, cf_ok, p2_ok = umark("new_masked", 1), umark("max", 1), umark("exp", 1), umark("coef", 1), umark("scaled", 1)
        tt_ok, tc_ok, pv2, ob_ok, of_ok, os_ok = umark("p_turned", 1), umark("p_out", 1), umark("pv", 1, credit=1), umark("o_out", 1), umark("o_folded", 1), umark("o_kept", 1, credit=1)
        ul = umark("dve_chain", 5)

        def satt_sync(sp, l):
            for dst, src in ((qT_s, Q_ROW), (kT_s, K_ROW), (vT_s, V_ROW), (g_s, DG_ROW)):
                sp.dma_start(dst[:, :, :], PT[bass.ds(l * COLS + src, 512), SEQ + 1:].rearrange("(h p) t -> p h t", p=P)).then_inc(u_in.sem, 16)
            for dst, src in ((n_m[0:NS], "nmask"), (fold[0:NS], "fold"), (u_cs[0:NS], "csel"), (onesP, "ones"), (ptab[:, :], "ptab")):
                sp.dma_start(dst, ins[src]).then_inc(u_in.sem, 16)
            sp.dma_start(u_lam[:, :, :], ins["lam"][bass.ds(l, 1)].rearrange("l p a b -> (l p) a b")).then_inc(u_in.sem, 16)
            sp.dma_start(u_sub[:, 0:3], ins["sub"][bass.ds(l, 1)].rearrange("l p a -> (l p) a")).then_inc(u_in.sem, 16)
            sp.wait_ge(u_in.sem, 16 * 11)
            with sp.Fori(0, 8) as b:
                pages = []
                for p in range(NP):
                    pg = sp.value_load(ptab[0:1, bass.ds(b * NP + p, 1)], min_val=0, max_val=N_PHYS - 1)
                    sp.wait_ge(kt_ok.sem, b * NP + (p + 1))
                    sp.dma_start(kpg[:, p % KS, :], ins["cache_k"][bass.ds(l * N_PHYS + pg, 1)].rearrange("n p c -> (n p) c")).then_inc(u_k[p % KS].sem, 16)
                    if p == 0:
                        pv2.wait_before(sp, b)
                    sp.dma_start(vpg[:, p, :], ins["cache_v"][bass.ds(l * N_PHYS + pg, 1)].rearrange("n p c -> (n p) c")).then_inc(u_v.sem, 16)


        def satt_scalar(act, l):
            kea.grant(act)
            act.wait_ge(u_in.sem, 16 * 11)
            act.wait_ge(u_lv.sem, 2)
            act.activation(u_lamv[:, 2:4], u_lamv[:, 0:2], ACT.Exp).then_inc(u_lv.sem, 1)
            act.wait_ge(u_pp.sem, 1)
            act.activation(vt_s[0:NS, :], bank[0][0:NS], ACT.Copy).then_inc(u_pa.sem, 1)
            act.wait_ge(u_q.sem, 2)
            act.sem_inc(tick, 1)
            with act.Fori(0, 8) as b:
                pv2.wait_before(act, b)
                qb_ok.inc(act.activation(qb[:, :, :], Qs[:, :, bass.ds(b, 1), :].rearrange("p h b t -> p h (b t)"), ACT.Copy))
                for p in range(0, NP, 2):
                    kt_ok.wait(act, b, p + 1)
                    if p % 4 == 0 and p >= 8:
                        sc2.wait(act, b, p // 4 - 1)
                    kea.inc(act.activation(kTs[:, (p // 4) % 2, :, (p % 4) * PG:(p % 4 + 1) * PG], bank[0].rearrange("p (h t) -> p h t", h=4), ACT.Copy))
                m_ok.wait(act, b, 1)
                e_ = act.activation(Pq[0:NS, :], psum[0:NS, 4:8, :], ACT.Exp, bias=u_st[0:NS, 2:3], scale=0.125, accum_out=u_st[0:NS, 3:4])
                e2_ok.inc(act.activation(Pn[0:NS, :], Pn[0:NS, :], ACT.Exp, bias=u_st[0:NS, 2:3], scale=0.125, accum_out=u_st[0:NS, 4:5]))
                cf_ok.wait(act, b, 1)
                act.activation(Pn[0:NS, :], Pn[0:NS, :], ACT.Copy, scale=u_st[0:NS, 6:7])
                p2_ok.inc(act.activation(Pq[0:NS, :], Pq[0:NS, :], ACT.Copy, scale=u_st[0:NS, 6:7]))
                tt_ok.wait(act, b, 1)
                act.activation(PTs[:, :, :], bank[0].rearrange("p (j r) -> p j r", j=NP), ACT.Copy)
                tc_ok.inc(act.activation(PTn[0:NS, :], bank[1][0:NS, 0:NS], ACT.Copy))
                pv2.wait(act, b, 1)
                ob_ok.inc(act.activation(Ob[0:NS, :], bank[2][0:NS], ACT.Copy))
                of_ok.wait(act, b, 1)
                os_ok.inc(act.activation(O_s[:, :, bass.ds(b * 4, 4)], diag(bank[0]), ACT.Copy))
                for m in (qb_ok, kea, e2_ok, p2_ok, tc_ok, ob_ok, os_ok):
                    m.close()
            act.wait_ge(u_pp.sem, 2)
            act.activation(ors[:, :, :], bank[0][:, 0:P].rearrange("p (c t) -> p c t", c=4), ACT.Sqrt, bias=u_lamv[:, 6:7], scale=1.0 / P).then_inc(u_pa.sem, 1)
            act.activation(sg_s[:, :, :], g_s[:, :, :], ACT.Tanh, scale=0.5).then_inc(u_pa.sem, 1)
            act.wait_ge(u_lv.sem, 14)
            act.dma_start(MT[RW:D, SEQ:TOK].rearrange("(h p) t -> p h t", p=P), omx[:, :, :]).then_inc(u_sto, 16)
            act.wait_ge(u_sto, 16)
        u_sto = psem("u_store")
        u_sems.append(u_sto)
        diag = lambda bk: bass.AP(bk.tensor, bk.offset, [list(bk.ap[0]), [20, 4], [1, 4]])

        def satt_vector(dve, l):
            ked.grant(dve)
            os_ok.grant(dve)
            pv2.grant(dve)
            n_ = [0]

            def lk(ins_, hold=True):
                n_[0] += 1
                ins_.then_inc(u_lv.sem, 1)
                if hold:
                    dve.wait_ge(u_lv.sem, n_[0])
            dve.memset(Qs[:, :, :, :], 0.0).then_inc(u_q.sem, 1)
            dve.wait_ge(u_q.sem, 1)
            dve.wait_ge(u_in.sem, 16 * 11)
            for a in range(2):
                for h in range(4):
                    r = slice(64 * a, 64 * a + 64)
                    q_ = dve.tensor_copy(Qs[r, h, :, 16 * a + 4 * h:16 * a + 4 * h + 4], qT_s[r, h, :].rearrange("p (b t) -> p b t", t=4))
            q_.then_inc(u_q.sem, 1)
            lk(dve.tensor_tensor(u_lam[:, 0:2, :], u_lam[:, 0:2, :], u_lam[:, 2:4, :], ALU.mult))
            lk(dve.tensor_reduce(u_lamv[:, 0:2], u_lam[:, 0:2, :], AX.X, ALU.add), False)
            dve.wait_ge(u_lv.sem, 3)
            n_[0] = 3
            lk(dve.tensor_tensor(u_lamv[:, 4:5], u_lamv[:, 3:4], u_lamv[:, 2:3], ALU.subtract))
            lk(dve.tensor_tensor(u_lamv[:, 5:6], u_lamv[:, 4:5], u_sub[:, 1:2], ALU.subtract))
            lk(dve.tensor_scalar(u_sub[:, 3:4], u_sub[:, 0:1], u_sub[:, 2:3], 0.5, ALU.mult, ALU.mult))
            lk(dve.tensor_scalar(u_st[0:NS, 8:9], u_cs[0:NS, 1:2], u_lamv[0:NS, 5:6], u_cs[0:NS, 0:1], ALU.mult, ALU.add))
            lk(dve.memset(u_lamv[:, 6:7], SUBLN_EPS))
            dve.sem_inc(tick, 1)
            with dve.Fori(0, 8) as b:
                for p in range(1, NP, 2):
                    kt_ok.wait(dve, b, p + 1)
                    if p % 4 == 1 and p >= 8:
                        sc2.wait(dve, b, p // 4 - 1)
                    ked.inc(dve.tensor_copy(kTs[:, (p // 4) % 2, :, (p % 4) * PG:(p % 4 + 1) * PG], bank[1].rearrange("p (h t) -> p h t", h=4)))
                scn.wait(dve, b, 1)
                p2 = dve.tensor_tensor(Pn[0:NS, :], bank[3][0:NS, 0:NS], n_m[0:NS, bass.ds(b, 1), :].rearrange("p b t -> p (b t)"), ALU.add)
                n_ok.link(dve, b, p2)
                dve.tensor_reduce(u_st[0:NS, 0:1], Pn[0:NS, :], AX.X, ALU.max)
                sc2.wait(dve, b, 4)
                ul.link(dve, b, dve.tensor_reduce(u_st[0:NS, 1:2], psum[0:NS, 4:8, :], AX.XY, ALU.max))
                ul.link(dve, b, dve.tensor_tensor(u_st[0:NS, 1:2], u_st[0:NS, 0:1], u_st[0:NS, 1:2], ALU.max))
                m_ok.inc(dve.tensor_scalar(u_st[0:NS, 2:3], u_st[0:NS, 1:2], -0.125, None, ALU.mult))
                e2_ok.wait(dve, b, 1)
                ul.link(dve, b, dve.tensor_tensor(u_st[0:NS, 5:6], u_st[0:NS, 3:4], u_st[0:NS, 4:5], ALU.add))
                ul.link(dve, b, dve.reciprocal(u_st[0:NS, 5:6], u_st[0:NS, 5:6]))
                cf_ok.inc(dve.tensor_tensor(u_st[0:NS, 6:7], u_st[0:NS, 5:6], u_st[0:NS, 8:9], ALU.mult))
                ul.inc(dve.tensor_copy(u_st[0:NS, 7:8], u_st[0:NS, 8:9]))
                for m in (ked, n_ok, m_ok, cf_ok, ul):
                    m.close()
            os_ok.wait(dve, 7, 1)
            n_[0] = 8
            lk(dve.tensor_tensor(osq_s[:, :, :], O_s[:, :, :], O_s[:, :, :], ALU.mult))
            dve.wait_ge(u_pa.sem, 3)
            lk(dve.reciprocal(ors[:, :, :], ors[:, :, :]))
            lk(dve.tensor_tensor(O_s[:, :, :], O_s[:, :, :], ors[:, :, :], ALU.mult))
            lk(dve.tensor_scalar(O_s[:, :, :], O_s[:, :, :], u_sub[:, 3:4], None, ALU.mult))
            lk(dve.scalar_tensor_tensor(sg_s[:, :, :], sg_s[:, :, :], 1.0, g_s[:, :, :], ALU.add, ALU.mult))
            lk(dve.tensor_tensor(omx[:, :, :], O_s[:, :, :], sg_s[:, :, :], ALU.mult))

        def satt_tensor(pe, l):
            kt_ok.grant(pe)
            pe.wait_ge(u_in.sem, 16 * 11)
            for h in range(4):
                mm = pe.transpose(bank[0][0:NS, h * P:(h + 1) * P], vT_s[:, h, :], ident[:, :])
            mm.then_inc(u_pp.sem, 1)
            pe.wait_ge(u_pa.sem, 1)
            pe.wait_ge(u_lv.sem, 1)
            pe.sem_inc(tick, 1)
            with pe.Fori(0, 8) as b:
                qb_ok.wait(pe, b, 1)
                for h in range(4):
                    mm = pe.matmul(bank[3][0:NS, 0:NS], qb[:, h, :], kT_s[:, h, :], start=(h == 0), stop=(h == 3))
                scn.inc(mm)

                def scores(g):
                    kea.wait(pe, b, 2 * g + 2)
                    ked.wait(pe, b, 2 * g + 2)
                    for h in range(4):
                        mm = pe.matmul(bank[4 + g][0:NS, :], qb[:, h, :], kTs[:, g % 2, h, :], start=(h == 0), stop=(h == 3))
                    sc2.inc(mm)
                for p in range(NP):
                    u_k[p % KS].wait(pe, b, p // KS + 1)
                    q = p // 2
                    if p % 2 == 0:
                        kea.wait_before(pe, b) if p == 0 else kea.wait(pe, b, q)
                        if p == 0:
                            os_ok.wait_before(pe, b)
                    else:
                        ked.wait_before(pe, b) if p == 1 else ked.wait(pe, b, q)
                    for h in range(4):
                        mm = pe.transpose(bank[p % 2][:, h * P:(h + 1) * P], kpg[:, p % KS, h * P:(h + 1) * P], ident[:, :])
                    kt_ok.inc(mm)
                    if p % 4 == 0 and p:
                        scores(p // 4 - 1)
                scores(3)
                p2_ok.wait(pe, b, 1)
                for j in range(NP):
                    pe.transpose(bank[0][:, j * NS:(j + 1) * NS], Pq[0:NS, j * PG:(j + 1) * PG], ident[0:NS, 0:NS])
                tt_ok.inc(pe.transpose(bank[1][0:NS, 0:NS], Pn[0:NS, :], ident[0:NS, 0:NS]))
                tc_ok.wait(pe, b, 1)
                pe.wait_ge(u_v.sem, (b + 1) * NP * 16)
                pe.sem_inc(tick, 1)
                for j in range(NP):
                    pe.matmul(bank[2][0:NS, :], PTs[:, j, :], vpg[:, j, :], start=(j == 0), stop=False)
                pv2.inc(pe.matmul(bank[2][0:NS, :], PTn[0:NS, :], vt_s[0:NS, :], start=False, stop=True))
                ob_ok.wait(pe, b, 1)
                for h in range(4):
                    mm = pe.matmul(bank[0][:, h * 16:(h + 1) * 16], Ob[0:NS, h * P:(h + 1) * P], fold[0:NS, :], start=True, stop=True)
                of_ok.inc(mm)
                for m in (scn, sc2, kt_ok, tt_ok, pv2, of_ok):
                    m.close()
            pe.wait_ge(u_lv.sem, 9)
            pe.matmul(bank[0][:, 0:P], onesP, osq_s[:, :, :], start=True, stop=True).then_inc(u_pp.sem, 1)

        Mark.pe, Mark.tick = nc.tensor, tick
        ph = Phases(nc, arrive, go, tick, [a_xs + [a_ssq, a_var, a_rstd, a_h, a_tr, a_ev, a_hi, a_nw], p_w + [p_w1, p_ws, p_z, p_mm, p_evA, p_evD] + p_st, r_sems, c_sems, t_sems, u_sems, d_sems], 7)
        block = ctx.enter_context(nc.Block())

        TILES = [(t, P) for t in range(NT)] + [(NT, NS)]

        @block.sync
        def _(sp):
            sp.dma_start(ident[:, :], ins["ident"]).then_inc(c_ld, 16)
            sp.dma_start(xcur[0:4 * P, :], x_in[0:4 * P, :]).then_inc(c_ld, 16)
            sp.dma_start(xcur[4 * P:TOK, :], x_in[4 * P:TOK, :]).then_inc(c_x, 16)
            sp.wait_ge(c_ld, 32)
            with sp.Fori(0, DEPTH) as l:
                sp.dma_start(nw[:, :], norm_w[bass.ds(l, 1)].rearrange("l p k -> (l p) k")).then_inc(a_nw, 16)
                for t, n in TILES:
                    if t == 4:
                        sp.wait_ge(c_x, 16)
                    if t >= 4:
                        sp.wait_ge(a_h, t - 3)
                    sp.dma_start(xt[0:n, t % 4, :], xcur[t * P:t * P + n, :]).then_inc(a_xs[t % 4], 16)
                ph.end(sp, l, 0, leader=True)
                with sp.Fori(0, CB // 3) as j:
                    for u in range(3):
                        sp.wait_ge(p_ws, j * 3 + (u + 1))
                        sp.dma_start(wb[u][:, :, :], w_in[bass.ds(l * CB + j * 3 + u, 1)].rearrange("c p k n -> (c p) k n")).then_inc(p_w[u], 16)
                ph.end(sp, l, 1, leader=True)
                rwkv_sync(sp, l)
                ph.end(sp, l, 2, leader=True)
                attn_sync(sp, l)
                ph.end(sp, l, 3, leader=True)
                rsmp_sync(sp, l)
                sp.dma_start(wo[:, :, :], ins["w_out"][bass.ds(l, 1)].rearrange("l p k n -> (l p) k n")).then_inc(d_cst, 16)
                sp.dma_start(fw[:, :], ins["fw"]).then_inc(d_cst, 16)
                ph.end(sp, l, 4, leader=True)
                satt_sync(sp, l)
                ph.end(sp, l, 5, leader=True)
                out_sync(sp, l)
                ph.end(sp, l, 6, leader=True)

        @block.scalar
        def _(act):
            act.wait_ge(c_ld, 32)
            act.wait_ge(c_eps, 2)
            with act.Fori(0, DEPTH) as l:
                act.wait_ge(c_ld, 32)

                def hi_part(t, n):
                    for q in range(2):
                        act.wait_ge(a_tr, t * 2 + q + 1)
                        act.activation(h_hi[:, 4 * q:4 * q + 4, t * P:t * P + n], bank[2 * (t % 2) + q].rearrange("p (k t) -> p k t", k=4)[:, :, 0:n], ACT.Copy).then_inc(a_hi, 1)
                for t, n in TILES:
                    act.wait_ge(a_ssq, t + 1)
                    act.activation(st[0:n, 1, t % 4:t % 4 + 1], st[0:n, 0, t % 4:t % 4 + 1], ACT.Sqrt, bias=eps_rms[0:n, :], scale=1.0 / D).then_inc(a_var, 1)
                    act.wait_ge(a_rstd, t + 1)
                    if t >= 2:
                        act.wait_ge(a_tr, (t - 1) * 2)
                    act.activation(ht[0:n, t % 2, :], xt[0:n, t % 4, :], ACT.Copy, scale=st[0:n, 2, t % 4:t % 4 + 1]).then_inc(a_h, 1)
                    if t:
                        hi_part(*TILES[t - 1])
                hi_part(*TILES[NT])
                ph.end(act, l, 0)
                act.sem_inc(p_evA, 3)
                act.wait_ge(p_z, 3)
                for s in p_st:
                    act.sem_inc(s, 16)
                with act.Fori(0, CB // 3) as j:
                    for u in range(3):
                        b = j * 3 + u
                        act.wait_ge(p_st[u], (j + 1) * 16)
                        for g in (0, 2, 4):
                            n = TG
                            act.wait_ge(p_mm, b * 5 + (g + 1 + 15))
                            act.activation(ost[u][:, 1 + g * TG:1 + g * TG + n], bank[g][:, 0:n], ACT.Copy).then_inc(p_evA, 1)
                        act.wait_ge(p_evA, (b + 2) * 3)
                        act.wait_ge(p_evD, (b + 2) * 2)
                        act.dma_start(PT[bass.ds(l * COLS + b * P, P), :], ost[u][:, :]).then_inc(p_st[u], 16)
                for u in range(3):
                    act.wait_ge(p_st[u], (CB // 3 + 1) * 16)
                ph.end(act, l, 1)
                rwkv_scalar(act, l)
                ph.end(act, l, 2)
                attn_scalar(act, l)
                ph.end(act, l, 3)
                rsmp_scalar(act, l)
                ph.end(act, l, 4)
                satt_scalar(act, l)
                ph.end(act, l, 5)
                out_scalar(act, l)
                ph.end(act, l, 6)

        @block.gpsimd
        def _(pool):
            pool.memset(eps_rms[:, :], RMS_EPS).then_inc(c_eps, 1)
            pool.memset(eps_gn[:, :], GN_EPS).then_inc(c_eps, 1)
            with pool.Fori(0, DEPTH) as l:
                pool.wait_ge(a_nw, 16)
                ph.end(pool, l, 0)
                pool.sem_inc(p_ws, 3)
                with pool.Fori(0, CB // 3) as j:
                    for u in range(3):
                        b = j * 3 + u
                        nwb = nw[:, :].unsqueeze(2).to_broadcast([P, KT, P])
                        pool.wait_ge(p_w[u], (j + 1) * 16)
                        pool.wait_ge(p_mm, b * 5 + 5)
                        pool.tensor_tensor(w_hi[u][:, :, :], wb[u][:, :, :], nwb, ALU.mult).then_inc(p_w1, 1)
                        pool.tensor_tensor(wb[u][:, :, :], wb[u][:, :, :], nwb, ALU.mult).then_inc(p_w1, 1)
                        pool.wait_ge(p_w1, (b + 1) * 2)
                        pool.tensor_tensor(w_lo[u][:, :, :], wb[u][:, :, :], w_hi[u][:, :, :].bitcast(F32), ALU.subtract).then_inc(p_ws, 1)
                ph.end(pool, l, 1)
                rwkv_gpsimd(pool, l)
                ph.end(pool, l, 2)
                ph.end(pool, l, 3)
                rsmp_gpsimd(pool, l)
                ph.end(pool, l, 4)
                ph.end(pool, l, 5)
                ph.end(pool, l, 6)

        @block.vector
        def _(dve):
            with dve.Fori(0, DEPTH) as l:

                def squares(t, n):
                    dve.wait_ge(a_xs[t % 4], (t // 4 + 1) * 16)
                    dve.scalar_tensor_tensor(sqj[0:n, :], xt[0:n, t % 4, :], 1.0, xt[0:n, t % 4, :], ALU.mult, ALU.mult, accum_out=st[0:n, 0, t % 4:t % 4 + 1]).then_inc(a_ssq, 1)

                def lo_part(t, n):
                    for q in range(2):
                        dve.wait_ge(a_hi, t * 2 + q + 1)
                        dve.tensor_tensor(h_lo[:, 4 * q:4 * q + 4, t * P:t * P + n], bank[2 * (t % 2) + q].rearrange("p (k t) -> p k t", k=4)[:, :, 0:n],
                                          h_hi[:, 4 * q:4 * q + 4, t * P:t * P + n].bitcast(F32), ALU.subtract).then_inc(a_ev, 1)
                squares(*TILES[0])
                for t, n in TILES:
                    dve.wait_ge(a_var, t + 1)
                    dve.reciprocal(st[0:n, 2, t % 4:t % 4 + 1], st[0:n, 1, t % 4:t % 4 + 1]).then_inc(a_rstd, 1)
                    if t < NT:
                        dve.wait_ge(a_ssq, t + 1)
                        squares(*TILES[t + 1])
                    if t:
                        lo_part(*TILES[t - 1])
                lo_part(*TILES[NT])
                ph.end(dve, l, 0)
                dve.sem_inc(p_evD, 2)
                for u in range(3):
                    dve.memset(ost[u][:, 0:1], 0.0).then_inc(p_z, 1)
                with dve.Fori(0, CB // 3) as j:
                    for u in range(3):
                        b = j * 3 + u
                        dve.wait_ge(p_st[u], (j + 1) * 16)
                        for g in (1, 3):
                            dve.wait_ge(p_mm, b * 5 + (g + 1 + 15))
                            dve.tensor_copy(ost[u][:, 1 + g * TG:1 + (g + 1) * TG], bank[g][:, 0:TG]).then_inc(p_evD, 1)
                ph.end(dve, l, 1)
                rwkv_vector(dve, l)
                ph.end(dve, l, 2)
                attn_vector(dve, l)
                ph.end(dve, l, 3)
                rsmp_vector(dve, l)
                ph.end(dve, l, 4)
                satt_vector(dve, l)
                ph.end(dve, l, 5)
                out_vector(dve, l)
                ph.end(dve, l, 6)

        @block.tensor
        def _(pe):
            pe.wait_ge(c_ld, 32)
            with pe.Fori(0, DEPTH) as l:
                for t, n in TILES:
                    pe.wait_ge(a_h, t + 1)
                    for q in range(2):
                        if t >= 2:
                            pe.wait_ge(a_ev, t * 2 + q - 3)
                        for k in range(4):
                            mm = pe.transpose(bank[2 * (t % 2) + q][:, k * P:k * P + n], ht[0:n, t % 2, (4 * q + k) * P:(4 * q + k + 1) * P], ident[0:n, 0:n])
                        mm.then_inc(a_tr, 1)
                ph.end(pe, l, 0)
                pe.sem_inc(p_mm, 15)
                with pe.Fori(0, CB // 3) as j:
                    for u in range(3):
                        b = j * 3 + u
                        pe.wait_ge(p_ws, b + 4)
                        for g in range(5):
                            if g % 2 == 0:
                                pe.wait_ge(p_evA, b * 3 + (g // 2 + 1))
                            else:
                                pe.wait_ge(p_evD, b * 2 + (g // 2 + 1))
                            col = slice(g * TG, (g + 1) * TG)
                            for k in range(KT):
                                pe.matmul(bank[g][:, 0:TG], w_hi[u][:, k, :], h_hi[:, k, col], start=(k == 0), stop=False)
                                pe.matmul(bank[g][:, 0:TG], w_hi[u][:, k, :], h_lo[:, k, col], start=False, stop=False)
                                mm = pe.matmul(bank[g][:, 0:TG], w_lo[u][:, k, :], h_hi[:, k, col], start=False, stop=(k == KT - 1))
                            mm.then_inc(p_mm, 1)
                ph.end(pe, l, 1)
                rwkv_tensor(pe, l)
                ph.end(pe, l, 2)
                attn_tensor(pe, l)
                ph.end(pe, l, 3)
                rsmp_tensor(pe, l)
                ph.end(pe, l, 4)
                satt_tensor(pe, l)
                ph.end(pe, l, 5)
                out_tensor(pe, l)
                ph.end(pe, l, 6)


_OUT = {"proj_t": (DEPTH * COLS, TOK + 1), "y": (TOK, D), "sp": (DEPTH * 512, 64), "ss": (DEPTH * 512, 8, 64)}


def kernel(**inputs):
    import numpy as np
    import concourse.bacc as bacc
    from concourse.bass_utils import run_bass_kernel_spmd as run

    f = {k: np.ascontiguousarray(v) for k, v in inputs.items()}
    arr = {}
    arr["x"] = np.concatenate([f["x_prompt"].reshape(SEQ, D), f["x_sample"].reshape(NS, D)], 0)
    arr["w_in"] = f["w_in"].reshape(DEPTH, KT, P, CB, P).transpose(0, 3, 2, 1, 4).reshape(DEPTH * CB, P, KT, P)
    arr["norm_w"] = f["norm_w"].reshape(DEPTH, KT, P).transpose(0, 2, 1)
    pr = np.zeros((DEPTH, RW, 16), np.float32)
    mu = f["shift_mu"]
    per = [mu[:, :RW], mu[:, RW:2 * RW], mu[:, 2 * RW:3 * RW], np.tile(mu[:, 3 * RW:], (1, 4)), f["decay_w0"], f["iclr_a0"],
           f["key_k"], f["key_a"], f["bonus_r_k"].reshape(DEPTH, RW), f["lnx_w"], f["lnx_b"]]
    for i, v in enumerate(per):
        pr[:, :, i] = v
    arr["prm"] = pr.reshape(DEPTH * 4, P, 16)
    lo = np.concatenate([f["decay_lora_b"], f["iclr_lora_b"]], 1)
    arr["lora"] = lo.reshape(DEPTH, P, 4, P).transpose(0, 2, 1, 3).reshape(DEPTH * 4, P, P)
    s_, t_ = np.arange(CH)[:, None], np.arange(CH)[None, :]
    c_ = lambda a: np.asarray(a, np.float32)
    arr["mS"] = c_(np.tile(np.concatenate([s_ <= t_, s_ < t_], 1), (2, 1)))
    arr["mR"] = c_(np.tile(np.arange(GRP) % CH != 0, (P, 1)))
    lower = lambda b: (s_ // (2 * b) == t_ // (2 * b)) & (s_ // b % 2 == 1) & (t_ // b % 2 == 0)
    two = lambda m: np.kron(np.eye(2), m)
    arr["mX1"] = c_(two(lower(1).T))
    arr["mL"] = c_(np.stack([two(lower(b)) for b in LEVELS], 1))
    lp = np.zeros((DEPTH, P, 4, 2, P), np.float32)
    lp[:, 0:64, :, 0] = f["decay_lora_b"].reshape(DEPTH, 64, 4, P)
    lp[:, 64:, :, 1] = f["iclr_lora_b"].reshape(DEPTH, 64, 4, P)
    arr["lorap"] = lp
    arr["eye"] = np.eye(CH, dtype=np.float32)
    arr["ones_b"] = c_(np.kron(np.eye(2), np.ones((64, 64))))
    arr["mean_b"] = c_(np.kron(np.eye(2), np.ones((64, 64)) / 64))
    lamc = np.stack([f["lam_q1"], f["lam_q2"], f["lam_k1"], f["lam_k2"]], 1)
    arr["lam"] = np.broadcast_to(lamc[:, None], (DEPTH, P, 4, 64))
    init = [0.8 - 0.6 * math.exp(-0.3 * l) for l in range(DEPTH)]
    arr["sub"] = np.stack([f["subln_w"]] + [c_(np.outer(v, np.ones(P))) for v in (init, [1 - a for a in init])], 2)
    q_, k_ = np.arange(P)[:, None], np.arange(P)[None, :]
    arr["dmask"] = c_(np.where(k_ <= q_, 0.0, NEG))
    arr["w_out"] = f["w_out"].reshape(DEPTH, KT, P, D).transpose(0, 2, 1, 3)
    arr["fw"] = np.broadcast_to(f["final_norm_w"][None], (P, D))
    arr["prev"] = f["state_shift"].reshape(DEPTH, 8, 13, P).transpose(0, 3, 2, 1)
    arr["mu13"] = f["shift_mu"].reshape(DEPTH, 13, P).transpose(0, 2, 1)
    arr["z0"] = f["state_rwkv"].reshape(DEPTH, 8, 4, 2, 64, 64).transpose(0, 3, 5, 2, 1, 4).reshape(DEPTH, P, 4, 8, 64)
    s_, t_ = np.arange(NS)[:, None], np.arange(NS)[None, :]
    same = s_ // 4 == t_ // 4
    arr["tmS"] = c_(np.tile(np.concatenate([same & (s_ <= t_), same & (s_ < t_)], 1), (2, 1)))
    arr["tmR"] = c_(np.tile(np.arange(P) % 4 != 0, (P, 1)))
    low = lambda b: (s_ // (2 * b) == t_ // (2 * b)) & (s_ // b % 2 == 1) & (t_ // b % 2 == 0)
    arr["tmX"] = c_(np.stack([low(1), low(1).T, low(2)], 1))
    arr["tbm"] = c_(np.tile(np.arange(NS)[:, None] // 4 == np.arange(8)[None, :], (2, 1)))
    arr["cache_k"] = f["cache_k"].reshape(DEPTH * N_PHYS, P, 512)
    arr["cache_v"] = f["cache_v"].reshape(DEPTH * N_PHYS, P, 512)
    arr["ptab"] = f["page_table"].reshape(1, P)
    row = np.arange(NS)[:, None, None]
    col, bb = np.arange(NS)[None, None, :], np.arange(8)[None, :, None]
    arr["nmask"] = c_(np.where((col // 4 == bb) & (col % 4 <= row % 4), 0.0, NEG))
    arr["fold"] = c_(np.tile(np.eye(16), (2, 1)))
    arr["csel"] = c_(np.stack([np.arange(NS) < 16, np.arange(NS) >= 16], 1))
    arr["ones"] = np.ones((P, P), np.float32)
    arr["ident"] = np.eye(P, dtype=np.float32)
    nc = bacc.Bacc("TRN2", target_bir_lowering=False, num_devices=1)
    arrays, ins, outs = {}, {}, {}
    for n, a in arr.items():
        a = np.ascontiguousarray(a)
        arrays["in_" + n] = a
        ins[n] = nc.dram_tensor("in_" + n, a.shape, mybir.dt.from_np(a.dtype), kind="ExternalInput").ap()
    for n, s in _OUT.items():
        outs[n] = nc.dram_tensor("out_" + n, s, F32, kind="ExternalOutput").ap()
    build(nc, ins, outs)
    r = run(nc, [arrays], core_ids=[0]).results[0]
    g = {n: r["out_" + n] for n in _OUT}
    pt = g["proj_t"].reshape(DEPTH, COLS, TOK + 1)
    kp = pt[:, 2688:3200, 1:SEQ + 1].reshape(DEPTH, 4, 128, 1, SEQ).transpose(0, 3, 4, 1, 2)
    ks = pt[:, 2688:3200, SEQ + 1:].reshape(DEPTH, 4, 128, 8, 4).transpose(0, 3, 4, 1, 2)
    vp = pt[:, 3200:3712, 1:SEQ + 1].reshape(DEPTH, 4, 128, 1, SEQ).transpose(0, 3, 4, 1, 2)
    vs = pt[:, 3200:3712, SEQ + 1:].reshape(DEPTH, 4, 128, 8, 4).transpose(0, 3, 4, 1, 2)
    hp = pt[:, :1664, SEQ].reshape(DEPTH, 1, 1664)
    hs = pt[:, :1664, SEQ + 1:].reshape(DEPTH, 1664, 8, 4)[:, :, :, 3].transpose(0, 2, 1)
    state = lambda a, b: a.reshape(DEPTH, 8, 64, b, 64).transpose(0, 3, 1, 4, 2)
    return (g["y"][:SEQ].reshape(1, SEQ, D), g["y"][SEQ:].reshape(8, 4, D), kp, vp, state(g["sp"], 1), hp,
            ks, vs, state(g["ss"], 8), hs)
```
